# Optimizing a Trainium2 kernel written in Bass

```python
import jax, jax.numpy as jnp
from jax import lax
import numpy as np

D_MODEL = 1024
BATCH = 1
SEQ = 1024
DEPTH = 1
DEC_BATCH = 8
DEC_SEQ = 16
PAST_LEN = 512

CHUNK = 64
H_RET = 8
RET_DK = 64
RET_DV = 64
RET_THETA = 10000.0
N_Q_HEADS = 8
N_KV_HEADS = 2
HEAD_DIM = 64
Q_PER_KV = N_Q_HEADS // N_KV_HEADS
WINDOW = 128
WIN_CHUNKS = WINDOW // CHUNK
ROPE_THETA = 500000.0
ROPE_DIM = HEAD_DIM // 4
MIX_WIDTH = H_RET * RET_DV + N_Q_HEADS * HEAD_DIM
IN_WIDTH = 2 * H_RET * RET_DK + 2 * H_RET * RET_DV + N_Q_HEADS * HEAD_DIM + 2 * N_KV_HEADS * HEAD_DIM
PEER_HEADS = 8
PEER_NKEYS = 128
PEER_EXPERTS = PEER_NKEYS * PEER_NKEYS
PEER_TOPK = 16
PEER_DKH = 128
PEER_BLOCK = 128
NORM_EPS = 1e-6
NEG_INF = -1e30

kernel_name = 'hybrid_retention_swa_peer_step'

def _rmsnorm(x, g):
    xf = x.astype(jnp.float32)
    y = xf * lax.rsqrt(jnp.mean(xf * xf, axis=-1, keepdims=True) + NORM_EPS)
    return (y * g.astype(jnp.float32)).astype(x.dtype)

def _rope(x, pos, rot_dim, theta):
    half = rot_dim // 2
    freqs = theta ** (-jnp.arange(half, dtype=jnp.float32) / half)
    ang = pos[:, None] * freqs[None, :]
    cos = jnp.cos(ang)[:, None, :]
    sin = jnp.sin(ang)[:, None, :]
    xf = x.astype(jnp.float32)
    x1 = xf[..., :half]
    x2 = xf[..., half:rot_dim]
    out = jnp.concatenate([x1 * cos - x2 * sin, x2 * cos + x1 * sin, xf[..., rot_dim:]], axis=-1)
    return out.astype(x.dtype)

def _in_proj(h, w_in, pos):
    B, T, _ = h.shape
    sizes = (H_RET * RET_DK, H_RET * RET_DK, H_RET * RET_DV, H_RET * RET_DV,
             N_Q_HEADS * HEAD_DIM, N_KV_HEADS * HEAD_DIM, N_KV_HEADS * HEAD_DIM)
    offsets = [int(v) for v in np.cumsum(sizes)[:-1]]
    z = h @ w_in
    qr, kr, vr, gr, qa, ka, va = jnp.split(z, offsets, axis=-1)
    qr = _rope(qr.reshape(B, T, H_RET, RET_DK), pos, RET_DK, RET_THETA)
    kr = _rope(kr.reshape(B, T, H_RET, RET_DK), pos, RET_DK, RET_THETA) * RET_DK ** -0.5
    vr = vr.reshape(B, T, H_RET, RET_DV)
    qa = _rope(qa.reshape(B, T, N_Q_HEADS, HEAD_DIM), pos, ROPE_DIM, ROPE_THETA)
    ka = _rope(ka.reshape(B, T, N_KV_HEADS, HEAD_DIM), pos, ROPE_DIM, ROPE_THETA)
    va = va.reshape(B, T, N_KV_HEADS, HEAD_DIM)
    return qr, kr, vr, gr, qa, ka, va

def _retention(q, k, v, s0, chunk):
    B, T, H, DK = q.shape
    DV = v.shape[-1]
    nc = T // chunk
    qc = q.astype(jnp.float32).reshape(B, nc, chunk, H, DK)
    kc = k.astype(jnp.float32).reshape(B, nc, chunk, H, DK)
    vc = v.astype(jnp.float32).reshape(B, nc, chunk, H, DV)
    log_g = jnp.log(1.0 - jnp.exp2(-5.0 - jnp.arange(H, dtype=jnp.float32)))
    idx = jnp.arange(chunk, dtype=jnp.float32)
    dist = jnp.abs(idx[:, None] - idx[None, :])
    decay_intra = jnp.exp(log_g[:, None, None] * dist)
    decay_q = jnp.exp(log_g[:, None] * (idx[None, :] + 1.0))
    decay_k = jnp.exp(log_g[:, None] * (chunk - 1.0 - idx[None, :]))
    decay_chunk = jnp.exp(log_g * chunk)
    scores = jnp.einsum('bnihd,bnjhd->bnhij', qc, kc) * decay_intra
    intra = jnp.einsum('bnhij,bnjhe->bnihe', scores, vc)
    kv = jnp.einsum('bnjhd,hj,bnjhe->nbhde', kc, decay_k, vc)

    def step(s, kv_n):
        return decay_chunk[None, :, None, None] * s + kv_n, s

    s_last, s_prev = lax.scan(step, s0.astype(jnp.float32), kv)
    inter = jnp.einsum('bnihd,nbhde,hi->bnihe', qc, s_prev, decay_q)
    o = (intra + inter).reshape(B, T, H, DV)
    return o, s_last

def _sink_attention(qb, kb, vb, valid, sinks):
    s = jnp.einsum('bnckgd,bnlkd->bnkgcl', qb, kb).astype(jnp.float32) * HEAD_DIM ** -0.5
    if valid is not None:
        s = jnp.where(valid[None, :, None, None, None, :], s, NEG_INF)
    sink = sinks.astype(jnp.float32).reshape(N_KV_HEADS, Q_PER_KV)[None, None, :, :, None, None]
    m = jnp.maximum(jnp.max(s, axis=-1, keepdims=True), sink)
    p = jnp.exp(s - m)
    denom = jnp.sum(p, axis=-1, keepdims=True) + jnp.exp(sink - m)
    return jnp.einsum('bnkgcl,bnlkd->bnckgd', p / denom, vb.astype(jnp.float32))

def _swa_prompt(q, k, v, sinks):
    B, T = q.shape[:2]
    nb = T // CHUNK
    qb = q.reshape(B, nb, CHUNK, N_KV_HEADS, Q_PER_KV, HEAD_DIM)
    pad = ((0, 0), (WINDOW, 0), (0, 0), (0, 0))
    kc = jnp.pad(k, pad).reshape(B, nb + WIN_CHUNKS, CHUNK, N_KV_HEADS, HEAD_DIM)
    vc = jnp.pad(v, pad).reshape(B, nb + WIN_CHUNKS, CHUNK, N_KV_HEADS, HEAD_DIM)
    kb = jnp.concatenate([kc[:, i:i + nb] for i in range(WIN_CHUNKS + 1)], axis=2)
    vb = jnp.concatenate([vc[:, i:i + nb] for i in range(WIN_CHUNKS + 1)], axis=2)
    key_pos = (jnp.arange(nb)[:, None] - WIN_CHUNKS) * CHUNK + jnp.arange((WIN_CHUNKS + 1) * CHUNK)[None, :]
    o = _sink_attention(qb, kb, vb, key_pos >= 0, sinks)
    return o.reshape(B, T, N_Q_HEADS * HEAD_DIM)

def _swa_sample(q, k, v, cache_k, cache_v, sinks):
    B, T = q.shape[:2]
    qb = q.reshape(B, 1, T, N_KV_HEADS, Q_PER_KV, HEAD_DIM)
    k_ctx = jnp.concatenate([cache_k.astype(k.dtype), k], axis=1)
    v_ctx = jnp.concatenate([cache_v.astype(v.dtype), v], axis=1)
    o = _sink_attention(qb, k_ctx[:, None], v_ctx[:, None], None, sinks)
    return o.reshape(B, T, N_Q_HEADS * HEAD_DIM), k_ctx[:, -WINDOW:], v_ctx[:, -WINDOW:]

def _merge(o_ret, gr, o_att, w_out, dtype):
    B, T = o_ret.shape[:2]
    mu = jnp.mean(o_ret, axis=-1, keepdims=True)
    var = jnp.mean(jnp.square(o_ret - mu), axis=-1, keepdims=True)
    o_r = ((o_ret - mu) * lax.rsqrt(var + NORM_EPS)).reshape(B, T, H_RET * RET_DV)
    o_r = jax.nn.silu(gr.astype(jnp.float32)) * o_r
    cat = jnp.concatenate([o_r, o_att], axis=-1).astype(dtype)
    return cat @ w_out

def _peer_tokens(h, w_q, keys, u_tab, v_tab):
    T = h.shape[0]
    q = (h @ w_q).reshape(T, PEER_HEADS, 2, PEER_DKH)
    s = jnp.einsum('tpsd,psnd->tpsn', q, keys).astype(jnp.float32)
    s1, i1 = lax.top_k(s[:, :, 0], PEER_TOPK)
    s2, i2 = lax.top_k(s[:, :, 1], PEER_TOPK)
    cand = (s1[..., :, None] + s2[..., None, :]).reshape(T, PEER_HEADS, PEER_TOPK * PEER_TOPK)
    cidx = (i1[..., :, None] * PEER_NKEYS + i2[..., None, :]).reshape(T, PEER_HEADS, PEER_TOPK * PEER_TOPK)
    sc, sel = lax.top_k(cand, PEER_TOPK)
    eidx = jnp.take_along_axis(cidx, sel, axis=-1)
    gate = jax.nn.softmax(sc, axis=-1)
    u = u_tab[eidx]
    act = jax.nn.gelu(jnp.einsum('td,tpkd->tpk', h, u).astype(jnp.float32))
    return jnp.einsum('tpk,tpkd->td', (gate * act).astype(h.dtype), v_tab[eidx])

def _peer(h, w_q, keys, u_tab, v_tab):
    shape = h.shape
    flat = h.reshape(-1, shape[-1])
    n = flat.shape[0]
    if n % PEER_BLOCK == 0 and n > PEER_BLOCK:
        blocks = flat.reshape(n // PEER_BLOCK, PEER_BLOCK, shape[-1])
        out = lax.map(lambda hb: _peer_tokens(hb, w_q, keys, u_tab, v_tab), blocks).reshape(n, shape[-1])
    else:
        out = _peer_tokens(flat, w_q, keys, u_tab, v_tab)
    return out.reshape(shape)

def setup_inputs(seed: int = 0) -> dict:
    key = jax.random.key(seed)
    ks = jax.random.split(key, 16)

    def nrm(k, shape, scale):
        return jax.random.normal(k, shape, jnp.float32) * scale

    return {
        'x_prompt': nrm(ks[0], (BATCH, SEQ, D_MODEL), 1.0),
        'x_sample': nrm(ks[1], (DEC_BATCH, DEC_SEQ, D_MODEL), 1.0),
        'state_ret': nrm(ks[2], (DEPTH, DEC_BATCH, H_RET, RET_DK, RET_DV), 0.5),
        'cache_swa_k': nrm(ks[3], (DEPTH, DEC_BATCH, WINDOW, N_KV_HEADS, HEAD_DIM), 1.0),
        'cache_swa_v': nrm(ks[4], (DEPTH, DEC_BATCH, WINDOW, N_KV_HEADS, HEAD_DIM), 1.0),
        'norm_mix': 1.0 + nrm(ks[5], (DEPTH, D_MODEL), 0.02),
        'w_in': nrm(ks[6], (DEPTH, D_MODEL, IN_WIDTH), D_MODEL ** -0.5),
        'attn_sinks': nrm(ks[7], (DEPTH, N_Q_HEADS), 0.5),
        'w_out': nrm(ks[8], (DEPTH, MIX_WIDTH, D_MODEL), MIX_WIDTH ** -0.5),
        'norm_ffn': 1.0 + nrm(ks[9], (DEPTH, D_MODEL), 0.02),
        'peer_w_q': nrm(ks[10], (DEPTH, D_MODEL, PEER_HEADS * 2 * PEER_DKH), D_MODEL ** -0.5),
        'peer_keys': nrm(ks[11], (DEPTH, PEER_HEADS, 2, PEER_NKEYS, PEER_DKH), PEER_DKH ** -0.5),
        'peer_u': nrm(ks[12], (DEPTH, PEER_EXPERTS, D_MODEL), D_MODEL ** -0.5),
        'peer_v': nrm(ks[13], (DEPTH, PEER_EXPERTS, D_MODEL), 0.5),
        'norm_final': 1.0 + nrm(ks[14], (D_MODEL,), 0.02),
    }

def reference(x_prompt, x_sample, state_ret, cache_swa_k, cache_swa_v, norm_mix, w_in, attn_sinks,
              w_out, norm_ffn, peer_w_q, peer_keys, peer_u, peer_v, norm_final):
    xp = x_prompt
    xs = x_sample
    Bp, Tp = xp.shape[:2]
    Bs, Ts = xs.shape[:2]
    pos_p = jnp.arange(Tp, dtype=jnp.float32)
    pos_s = jnp.arange(Ts, dtype=jnp.float32) + PAST_LEN
    ret_p, k_p, v_p, ret_s, k_s, v_s = [], [], [], [], [], []
    for l in range(DEPTH):
        h = _rmsnorm(xp, norm_mix[l])
        qr, kr, vr, gr, qa, ka, va = _in_proj(h, w_in[l], pos_p)
        s0 = jnp.zeros((Bp, H_RET, RET_DK, RET_DV), jnp.float32)
        o_ret, s_last = _retention(qr, kr, vr, s0, CHUNK)
        o_att = _swa_prompt(qa, ka, va, attn_sinks[l])
        xp = xp + _merge(o_ret, gr, o_att, w_out[l], xp.dtype)
        xp = xp + _peer(_rmsnorm(xp, norm_ffn[l]), peer_w_q[l], peer_keys[l], peer_u[l], peer_v[l])
        ret_p.append(s_last)
        k_p.append(ka[:, -WINDOW:])
        v_p.append(va[:, -WINDOW:])
        h = _rmsnorm(xs, norm_mix[l])
        qr, kr, vr, gr, qa, ka, va = _in_proj(h, w_in[l], pos_s)
        o_ret, s_last = _retention(qr, kr, vr, state_ret[l], Ts)
        o_att, k_buf, v_buf = _swa_sample(qa, ka, va, cache_swa_k[l], cache_swa_v[l], attn_sinks[l])
        xs = xs + _merge(o_ret, gr, o_att, w_out[l], xs.dtype)
        xs = xs + _peer(_rmsnorm(xs, norm_ffn[l]), peer_w_q[l], peer_keys[l], peer_u[l], peer_v[l])
        ret_s.append(s_last)
        k_s.append(k_buf)
        v_s.append(v_buf)
    y_prompt = _rmsnorm(xp, norm_final)
    y_sample = _rmsnorm(xs, norm_final)
    new_state_ret_prompt = jnp.stack(ret_p, axis=0)
    new_cache_swa_k_prompt = jnp.stack(k_p, axis=0)
    new_cache_swa_v_prompt = jnp.stack(v_p, axis=0)
    new_state_ret_sample = jnp.stack(ret_s, axis=0)
    new_cache_swa_k_sample = jnp.stack(k_s, axis=0)
    new_cache_swa_v_sample = jnp.stack(v_s, axis=0)
    return (y_prompt, y_sample, new_state_ret_prompt, new_cache_swa_k_prompt, new_cache_swa_v_prompt,
            new_state_ret_sample, new_cache_swa_k_sample, new_cache_swa_v_sample)


_drawn_inputs = setup_inputs


def setup_inputs(seed=0):
    import zlib

    import numpy as np

    out = dict(_drawn_inputs(seed))
    spreads = {}
    factors = {'attn_sinks': 52.097, 'norm_final': 8.237}
    for name, (base, spread) in spreads.items():
        noise = np.random.default_rng([zlib.crc32(name.encode()), seed]).standard_normal(out[name].shape)
        drawn = base * np.exp(spread * noise) if base else spread * noise
        out[name] = __import__('jax').numpy.asarray(drawn.astype(out[name].dtype))
    for name, factor in factors.items():
        out[name] = (out[name] * factor).astype(out[name].dtype)
    return out
```

```python
from contextlib import ExitStack

import numpy as np

import concourse.bass as bass
from concourse import mybir

F32 = mybir.dt.float32
F32R = mybir.dt.float32r
U32 = mybir.dt.uint32
ALU = mybir.AluOpType
ACT = mybir.ActivationFunctionType
AX = mybir.AxisListType

P = 128
D = 1024
KC = D // P
SEQ = 1024
STREAMS = 8
DEC = 16
PAST = 512
PROMPT_TILES = SEQ // P
TILES = PROMPT_TILES + 1
SAMPLE = PROMPT_TILES
TOKENS = TILES * P
HEADS = 8
PAIRS = HEADS // 2
HD = 64
KV = 2
CHUNK = 64
WINDOW = 128
IN_W = 2816
EPS = 1e-6
RET_THETA = 10000.0
ROPE_THETA = 500000.0
ROPE_DIM = HD // 4
NEG = -1e30
LOWEST = -3.0e38

Z_Q, Z_K, Z_V, Z_G, Z_QA, Z_KA, Z_VA = 0, 512, 1024, 1536, 2048, 2560, 2688
BANK = 512

PEER_HEADS = 8
SIDES = 2 * PEER_HEADS
NKEYS = 128
TOPK = 16
CHOSEN = PEER_HEADS * TOPK
BLOCKS = 3
BT = TILES // BLOCKS
BTOK = BT * P

T_C, T_S, T_CA, T_SA, T_MASK, T_COLS = 0, 64, 128, 144, 160, 416
M_MASK, M_DQ, M_DK, M_G, M_COLS = 0, 1024, 1536, 1544, 1548


def rope_tables(pos, rot, theta):
    half = rot // 2
    freqs = np.float32(theta) ** (-np.arange(half, dtype=np.float32) / np.float32(half))
    ang = pos[:, None] * freqs[None, :]
    c, s = np.cos(ang), np.sin(ang)
    return np.concatenate([c, c], 1), np.concatenate([-s, s], 1)


def tile_tables():
    pos = np.concatenate([np.arange(SEQ), PAST + np.arange(P) % DEC]).astype(np.float32)
    out = np.zeros((TILES, P, T_COLS), np.float32)
    c, s = rope_tables(pos, HD, RET_THETA)
    out[:, :, T_C:T_C + 64] = c.reshape(TILES, P, 64)
    out[:, :, T_S:T_S + 64] = s.reshape(TILES, P, 64)
    c, s = rope_tables(pos, ROPE_DIM, ROPE_THETA)
    out[:, :, T_CA:T_CA + 16] = c.reshape(TILES, P, 16)
    out[:, :, T_SA:T_SA + 16] = s.reshape(TILES, P, 16)
    q = np.arange(P)[:, None]
    k = np.arange(2 * P)[None, :]
    qc, kc = q // CHUNK + 2, k // CHUNK
    seen = (kc <= qc) & (kc >= qc - WINDOW // CHUNK)
    out[1:PROMPT_TILES, :, T_MASK:] = np.where(seen, 0, NEG)
    out[0, :, T_MASK:] = np.where(seen & (k >= P), 0, NEG)
    own = (k < P) | ((k - P) // DEC == q // DEC)
    out[SAMPLE, :, T_MASK:] = np.where(own, 0, NEG)
    return out


def mode_tables():
    log_g = np.log1p(-np.exp2(-5.0 - np.arange(HEADS)))
    i = np.arange(P)
    out = np.zeros((2, P, M_COLS), np.float32)
    for mode, span in enumerate((P, DEC)):
        chunk = CHUNK if mode == 0 else DEC
        j_, i_ = i[:, None], i[None, :]
        if mode == 0:
            seen = (j_ // chunk <= i_ // chunk)
        else:
            seen = (j_ // chunk == i_ // chunk)
        for h in range(HEADS):
            p, r = h // 2, h % 2
            m = np.where(seen, np.exp(log_g[h] * np.abs(i_ - j_)), 0) * HD ** -0.5
            out[mode, :, M_MASK + (r * 4 + p) * P:M_MASK + (r * 4 + p + 1) * P] = m
            dq = np.exp(log_g[h] * (i % span + 1.0))
            out[mode, 64 * r:64 * r + 64, M_DQ + p * P:M_DQ + (p + 1) * P] = dq[None, :]
            out[mode, :, M_DK + h] = np.exp(log_g[h] * (span - 1.0 - i % span)) * HD ** -0.5
            out[mode, 64 * r:64 * r + 64, M_G + p] = np.exp(log_g[h] * span)
    return out


def spread(ap, axis, n):
    a = ap.unsqueeze(axis)
    shape = list(a.shape)
    shape[axis] = n
    return a.to_broadcast(shape)


class Chain:

    def __init__(self, eng, sem, base=0):
        self.eng, self.sem, self.base, self.n = eng, sem, base, 0

    def after(self, ins):
        self.n += 1
        ins.then_inc(self.sem, 1)
        self.eng.wait_ge(self.sem, self.base + self.n)


def stage_mix(nc, psum, dr):
    X, TAB, MODE, WIN, WOUT = dr["x"], dr["tile_tab"], dr["mode_tab"], dr["w_in"], dr["w_out"]
    with ExitStack() as ctx:
        def sb(name, shape, dt=F32):
            return ctx.enter_context(nc.sbuf_tensor(name + "_sb", shape, dt))

        def sem(name):
            return ctx.enter_context(nc.semaphore(name))

        w_in = sb("w_in", [P, KC * IN_W])
        w_inv = w_in[:, :].rearrange("p (k n) -> p k n", k=KC)
        w_out = sb("w_out", [P, KC, D])
        ident = sb("ident", [P, P])
        gain = sb("gain_mix", [P, D])
        sinks = sb("sinks", [P, HEADS])
        mode = sb("mode", [P, M_COLS])
        tab = sb("tab", [P, T_COLS])
        xt = sb("xt", [P, D])
        h = sb("h", [P, D])
        hT = sb("hT", [P, KC, P])
        zs = sb("zs", [P, IN_W])
        qk = sb("qk", [P, 1024])
        rot = sb("rot", [P, 1024])
        kd = sb("kd", [P, 512])
        kad = sb("kad", [P, KV, 2, HD])
        rota = sb("rota", [P, 10, 16])
        rotb = sb("rotb", [P, 10, 16])
        qT = sb("qT", [P, PAIRS, P])
        qTd = sb("qTd", [P, PAIRS, P])
        kT = sb("kT", [P, PAIRS, P])
        qaT = sb("qaT", [P, PAIRS, P])
        kaT = sb("kaT", [P, KV, 2, P])
        v_prev = sb("v_prev", [P, P])
        scT = sb("scT", [P, 2, PAIRS, P])
        S = sb("S", [P, PAIRS, P])
        sm = sb("sm", [P, HEADS, 2 * P])
        pT = sb("pT", [P, 2, HEADS, P])
        cat = sb("cat", [P, D])
        catT = hT
        ss = sb("ss", [P, 1])
        std = sb("std", [P, 1])
        rstd = sb("rstd", [P, 1])
        gsum = sb("gsum", [P, HEADS])
        gvar = sb("gvar", [P, HEADS])
        gstd = sb("gstd", [P, HEADS])
        grstd = sb("grstd", [P, HEADS])
        mx = sb("mx", [P, HEADS])
        nmx = sb("nmx", [P, HEADS])
        sk = sb("sk", [P, HEADS])
        ske = sb("ske", [P, HEADS])
        den = sb("den", [P, HEADS])
        rden = sb("rden", [P, HEADS])
        dev = h[:, 0:512]
        dsq = h[:, 512:1024]
        x1t = rot

        def over(at, n):
            return w_in[:, at:at + n]

        kcT = over(0, 2048).rearrange("p (k b w) -> p k b w", k=KV, b=STREAMS)
        vc = over(2048, 1024).rearrange("p (b e) -> p b e", b=STREAMS)
        S0 = over(3072, 4096).rearrange("p (q b e) -> p q b e", q=PAIRS, b=STREAMS)
        qaTm = over(7168, 4096).rearrange("p (q b t) -> p q b t", q=PAIRS, b=STREAMS)
        qTdm = over(11264, 4096).rearrange("p (q b t) -> p q b t", q=PAIRS, b=STREAMS)
        vm = over(15360, 4096).rearrange("p (h b e) -> p h b e", h=HEADS, b=STREAMS)
        pTm = over(19456, 2048).rearrange("p (s b t) -> p s b t", s=2, b=STREAMS)
        bmask = over(21504, STREAMS)

        weights_loaded = sem("weights_loaded")
        w_out_loaded = sem("w_out_loaded")
        const_loaded = sem("const_loaded")
        mode_loaded = sem("mode_loaded")
        sample_loaded = sem("sample_loaded")
        x_loaded = sem("x_loaded")
        tab_loaded = sem("tab_loaded")
        ident_made = sem("ident_made")
        init_done = sem("init_done")
        act_step = sem("act_step")
        dve_step = sem("dve_step")
        std_ready = sem("std_ready")
        h_ready = sem("h_ready")
        hT_psum = sem("hT_psum")
        hT_ready = sem("hT_ready")
        z_psum = sem("z_psum")
        zs_ready = sem("zs_ready")
        rot_ready = sem("rot_ready")
        rota_ready = sem("rota_ready")
        qk_psum = sem("qk_psum")
        qkT_ready = sem("qkT_ready")
        qTd_ready = sem("qTd_ready")
        sc_psum = sem("sc_psum")
        scT_ready = sem("scT_ready")
        o_psum = sem("o_psum")
        st_psum = sem("st_psum")
        S_ready = sem("S_ready")
        gvar_ready = sem("gvar_ready")
        gstd_ready = sem("gstd_ready")
        sw_psum = sem("sw_psum")
        mx_ready = sem("mx_ready")
        p_ready = sem("p_ready")
        ske_ready = sem("ske_ready")
        pT_psum = sem("pT_psum")
        pT_ready = sem("pT_ready")
        pTm_ready = sem("pTm_ready")
        pTm_used = sem("pTm_used")
        oa_psum = sem("oa_psum")
        cat_ready = sem("cat_ready")
        catT_psum = sem("catT_psum")
        catT_ready = sem("catT_ready")
        y_psum = sem("y_psum")
        x1_ready = sem("x1_ready")
        x1_stored = sem("x1_stored")
        shifted = sem("shifted")
        masked_ready = sem("masked_ready")
        zeroed = sem("zeroed")
        out_stored = sem("out_stored")

        block = ctx.enter_context(nc.Block())

        @block.gpsimd
        def _(eng):
            eng.memset(ident[:, :], 0.0).then_inc(ident_made, 1)
            eng.wait_ge(ident_made, 1)
            eng.affine_select(out=ident[:, :], in_=ident[:, :], compare_op=ALU.not_equal, fill=1.0, base=0,
                              pattern=[[-1, P]], channel_multiplier=1).then_inc(ident_made, 1)
            eng.memset(S[:, :, :], 0.0).then_inc(init_done, 1)
            eng.memset(kaT[:, :, :, :], 0.0).then_inc(init_done, 1)
            eng.memset(v_prev[:, :], 0.0).then_inc(init_done, 1)
            eng.wait_ge(z_psum, 6 * TILES)
            eng.memset(qaTm, 0.0).then_inc(zeroed, 1)
            eng.memset(qTdm, 0.0).then_inc(zeroed, 1)
            eng.memset(pTm, 0.0).then_inc(zeroed, 1)
            eng.memset(S0, 0.0).then_inc(zeroed, 1)
            eng.memset(bmask, 1.0).then_inc(zeroed, 1)
            eng.wait_ge(zeroed, 5)
            eng.affine_select(out=bmask, in_=bmask, compare_op=ALU.is_ge, fill=0.0, base=0,
                              pattern=[[-DEC, STREAMS]], channel_multiplier=1).then_inc(zeroed, 1)
            eng.wait_ge(zeroed, 6)
            eng.affine_select(out=bmask, in_=bmask, compare_op=ALU.is_ge, fill=0.0, base=DEC - 1,
                              pattern=[[DEC, STREAMS]], channel_multiplier=-1).then_inc(zeroed, 1)

        @block.sync
        def _(eng):
            def tile_in(t):
                eng.wait_ge(x1_ready, t)
                eng.dma_start(xt[:, :], X[t]).then_inc(x_loaded, 16)
                eng.dma_start(tab[:, :], TAB[t]).then_inc(tab_loaded, 16)

            def tile_out(t):
                eng.wait_ge(x1_ready, t + 1)
                eng.dma_start(dr["x1"][t], x1t[:, :]).then_inc(x1_stored, 16)

            eng.dma_start(gain[:, :], dr["norm_mix"].partition_broadcast(P)).then_inc(const_loaded, 16)
            eng.dma_start(sinks[:, :], dr["sinks"].partition_broadcast(P)).then_inc(const_loaded, 16)
            eng.dma_start(mode[:, :], MODE[0]).then_inc(mode_loaded, 16)
            with eng.Fori(0, PROMPT_TILES) as t:
                tile_in(t)
                tile_out(t)
            eng.dma_start(dr["o_kp"], zs[:, Z_KA:Z_VA]).then_inc(out_stored, 16)
            eng.dma_start(dr["o_vp"], zs[:, Z_VA:IN_W]).then_inc(out_stored, 16)
            for r in range(2):
                eng.dma_start(dr["o_sp"].rearrange("(q r) d e -> r d q e", r=2)[r],
                              S[64 * r:64 * r + 64, :, 64 * r:64 * r + 64]).then_inc(out_stored, 16)
            eng.dma_start(mode[:, :], MODE[1]).then_inc(mode_loaded, 16)
            eng.wait_ge(out_stored, 64)
            tile_in(SAMPLE)
            eng.wait_ge(z_psum, 6 * TILES)
            for r in range(2):
                eng.dma_start(kcT[64 * r:64 * r + 64], dr["kcT"]).then_inc(sample_loaded, 16)
            eng.wait_ge(zeroed, 5)
            for r in range(2):
                for q in range(PAIRS):
                    eng.dma_start(S0[64 * r:64 * r + 64, q, :, 64 * r:64 * r + 64], dr["s0"][r, :, q])\
                       .then_inc(sample_loaded, 16)
            eng.dma_start(vc, dr["vc"].rearrange("b w e -> w b e")).then_inc(sample_loaded, 16)
            eng.dma_start(dr["o_ks"][:, 0:WINDOW - DEC, :], dr["kc"][:, DEC:WINDOW, :]).then_inc(out_stored, 16)
            eng.dma_start(dr["o_vs"][:, 0:WINDOW - DEC, :], dr["vc"][:, DEC:WINDOW, :]).then_inc(out_stored, 16)
            eng.wait_ge(rota_ready, 2 * TILES)
            for b in range(STREAMS):
                eng.dma_start(dr["o_ks"][b, WINDOW - DEC:, :], zs[DEC * b:DEC * (b + 1), Z_KA:Z_VA])\
                   .then_inc(out_stored, 16)
                eng.dma_start(dr["o_vs"][b, WINDOW - DEC:, :], zs[DEC * b:DEC * (b + 1), Z_VA:IN_W])\
                   .then_inc(out_stored, 16)
            eng.wait_ge(S_ready, 8 * TILES)
            for r in range(2):
                for q in range(PAIRS):
                    eng.dma_start(dr["o_ss"][r, :, q], S0[64 * r:64 * r + 64, q, :, 64 * r:64 * r + 64])\
                       .then_inc(out_stored, 16)
            tile_out(SAMPLE)
            eng.wait_ge(x1_stored, 16 * TILES)
            eng.wait_ge(out_stored, 16 * (4 + 2 + 2 * STREAMS + 2 * PAIRS))

        @block.tensor
        def _(eng):
            def bank(b, n=1):
                return psum[:, b * BANK:(b + n) * BANK]

            def tile(t, sample):
                eng.wait_ge(h_ready, t + 1)
                for k in range(KC):
                    mm = eng.transpose(bank(6, 2)[:, k * P:(k + 1) * P], h[:, k * P:(k + 1) * P], ident[:, :])
                mm.then_inc(hT_psum, 1)
                eng.wait_ge(hT_ready, t + 1)
                for b, n in enumerate((0, 1, 4, 5, 2, 3)):
                    w = min(BANK, IN_W - n * BANK)
                    for k in range(KC):
                        mm = eng.matmul(bank(b)[:, 0:w], hT[:, k, :], w_inv[:, k, n * BANK:n * BANK + w],
                                        start=(k == 0), stop=(k == KC - 1))
                    mm.then_inc(z_psum, 1)
                eng.wait_ge(rot_ready, 2 * t + 2)
                for g in range(2):
                    for q in range(PAIRS):
                        mm = eng.transpose(bank(6 + g)[:, q * P:(q + 1) * P],
                                           qk[:, g * 512 + q * P:g * 512 + (q + 1) * P], ident[:, :])
                    mm.then_inc(qk_psum, 1)
                eng.wait_ge(rota_ready, 2 * t + 2)
                eng.wait_ge(zs_ready, 6 * t + 6)
                for q in range(PAIRS):
                    mm = eng.transpose(bank(0)[:, q * P:(q + 1) * P], zs[:, Z_QA + q * P:Z_QA + (q + 1) * P],
                                       ident[:, :])
                mm.then_inc(qk_psum, 1)
                for g in range(KV):
                    mm = eng.transpose(bank(1)[:, g * P:(g + 1) * P],
                                       kad[:, g, :, :].rearrange("p c e -> p (c e)"), ident[:, :])
                mm.then_inc(qk_psum, 1)
                eng.wait_ge(qkT_ready, 4 * t + 4)
                for r in range(2):
                    for q in range(PAIRS):
                        s = slice(64 * r, 64 * r + 64)
                        mm = eng.matmul(bank(2 + r)[:, q * P:(q + 1) * P], kT[s, q, :], qT[s, q, :],
                                        start=True, stop=True)
                mm.then_inc(sc_psum, 1)
                if sample:
                    eng.wait_ge(masked_ready, 2)
                    eng.wait_ge(sample_loaded, 16 * (3 + 2 * PAIRS))
                for r in range(2):
                    for q in range(PAIRS):
                        s = slice(64 * r, 64 * r + 64)
                        out = bank((6, 0)[r], 2)[:, q * 256:(q + 1) * 256]
                        if not sample:
                            mm = eng.matmul(out, qaT[s, q, :], kaT[s, q // 2, :, :].rearrange("p c t -> p (c t)"),
                                            start=True, stop=True)
                        else:
                            for b in range(STREAMS):
                                eng.matmul(out[:, 0:P], qaTm[s, q, b, :], kcT[s, q // 2, b, :],
                                           start=(b == 0), stop=(b == STREAMS - 1))
                            mm = eng.matmul(out[:, P:2 * P], qaT[s, q, :], kaT[s, q // 2, 1, :],
                                            start=True, stop=True)
                mm.then_inc(sw_psum, 1)
                eng.wait_ge(rot_ready, 2 * t + 2)
                if not sample:
                    for q in range(PAIRS):
                        mm = eng.matmul(bank(5)[:, q * P:(q + 1) * P], kd[:, q * P:(q + 1) * P],
                                        zs[:, Z_V + q * P:Z_V + (q + 1) * P], start=True, stop=True)
                    mm.then_inc(st_psum, 1)
                eng.wait_ge(scT_ready, t + 1)
                eng.wait_ge(qTd_ready, t + 1)
                if sample:
                    eng.wait_ge(masked_ready, 2)
                else:
                    eng.wait_ge(S_ready, 8 * t)
                for q in range(PAIRS):
                    out = bank(4)[:, q * P:(q + 1) * P]
                    if not sample:
                        eng.matmul(out, qTd[:, q, :], S[:, q, :], start=True, stop=False)
                    else:
                        for b in range(STREAMS):
                            eng.matmul(out, qTdm[:, q, b, :], S0[:, q, b, :], start=(b == 0), stop=False)
                    for r in range(2):
                        hh = 2 * q + r
                        mm = eng.matmul(out[:, r * HD:(r + 1) * HD], scT[:, r, q, :],
                                        zs[:, Z_V + hh * HD:Z_V + (hh + 1) * HD], start=False, stop=(r == 1))
                mm.then_inc(o_psum, 1)
                if sample:
                    eng.wait_ge(masked_ready, 3)
                    for hh in range(HEADS):
                        q = hh // 2
                        if hh >= 1:
                            eng.wait_ge(S_ready, 8 * t + hh)
                        eng.matmul(bank(5), kd[:, q * P:(q + 1) * P],
                                   vm[:, hh].rearrange("p b e -> p (b e)"), start=True, stop=True)\
                           .then_inc(st_psum, 1)
                for c in range(2):
                    for i in range(HEADS):
                        if c == 0:
                            eng.wait_ge(p_ready, 8 * t + i + 1)
                        mm = eng.transpose(bank((2, 6)[c], 2)[:, i * P:(i + 1) * P],
                                           sm[:, i, c * P:(c + 1) * P], ident[:, :])
                    mm.then_inc(pT_psum, 1)
                eng.wait_ge(pT_ready, 2 * t + 2)
                for hh in range(HEADS):
                    q, r = hh // 2, hh % 2
                    i, g = r * PAIRS + q, hh // 4
                    out = bank(0)[:, hh * HD:(hh + 1) * HD]
                    if not sample:
                        eng.matmul(out, pT[:, 0, i, :], v_prev[:, g * HD:(g + 1) * HD], start=True, stop=False)
                    else:
                        eng.wait_ge(pTm_ready, hh + 1)
                        for b in range(STREAMS):
                            mm = eng.matmul(out, pTm[:, hh % 2, b, :], vc[:, b, g * HD:(g + 1) * HD],
                                            start=(b == 0), stop=False)
                        mm.then_inc(pTm_used, 1)
                    mm = eng.matmul(out, pT[:, 1, i, :], zs[:, Z_VA + g * HD:Z_VA + (g + 1) * HD],
                                    start=False, stop=True)
                mm.then_inc(oa_psum, 1)
                eng.wait_ge(cat_ready, t + 1)
                for k in range(KC):
                    mm = eng.transpose(bank(4, 2)[:, k * P:(k + 1) * P], cat[:, k * P:(k + 1) * P], ident[:, :])
                mm.then_inc(catT_psum, 1)
                eng.wait_ge(catT_ready, t + 1)
                for n in range(2):
                    for k in range(KC):
                        mm = eng.matmul(bank(2 + n), catT[:, k, :], w_out[:, k, n * BANK:(n + 1) * BANK],
                                        start=(k == 0), stop=(k == KC - 1))
                mm.then_inc(y_psum, 1)

            eng.wait_ge(ident_made, 2)
            eng.wait_ge(init_done, 3)
            eng.wait_ge(weights_loaded, 16)
            eng.wait_ge(w_out_loaded, 16)
            with eng.Fori(0, PROMPT_TILES) as t:
                tile(t, False)
            tile(SAMPLE, True)

        @block.scalar
        def _(eng):
            def tile(t, sample):
                eng.wait_ge(x_loaded, 16 * t + 16)
                chain = Chain(eng, act_step, t)
                chain.after(eng.activation(cat[:, :], xt[:, :], ACT.Square, accum_out=ss[:, :]))
                eng.activation(std[:, :], ss[:, :], ACT.Sqrt, bias=EPS, scale=1.0 / D).then_inc(std_ready, 1)
                eng.wait_ge(hT_psum, t + 1)
                eng.copy(hT[:, :, :].rearrange("p k t -> p (k t)"), psum[:, 6 * BANK:8 * BANK])\
                   .then_inc(hT_ready, 1)
                for b, n in enumerate((0, 1, 4, 5, 2, 3)):
                    w = min(BANK, IN_W - n * BANK)
                    eng.wait_ge(z_psum, 6 * t + b + 1)
                    if b == 3:
                        eng.wait_ge(shifted, t)
                    eng.activation(zs[:, n * BANK:n * BANK + w], psum[:, b * BANK:b * BANK + w],
                                   ACT.Silu if n == 3 else ACT.Copy).then_inc(zs_ready, 1)
                for i, (src, dst) in enumerate(((6, qT), (7, kT), (0, qaT))):
                    eng.wait_ge(qk_psum, 4 * t + i + 1)
                    eng.copy(dst[:, :, :].rearrange("p q t -> p (q t)"), psum[:, src * BANK:(src + 1) * BANK])\
                       .then_inc(qkT_ready, 1)
                eng.wait_ge(qk_psum, 4 * t + 4)
                eng.copy(kaT[:, :, 1, :], psum[:, BANK:BANK + 256].rearrange("p (g t) -> p g t", g=KV))\
                   .then_inc(qkT_ready, 1)
                eng.wait_ge(gvar_ready, t + 1)
                eng.activation(gstd[:, :], gvar[:, :], ACT.Sqrt, bias=EPS, scale=1.0 / HD).then_inc(gstd_ready, 1)
                eng.wait_ge(mx_ready, t + 1)
                for i in range(HEADS):
                    eng.activation(sm[:, i, :], sm[:, i, :], ACT.Exp, bias=nmx[:, i:i + 1],
                                   accum_out=den[:, i:i + 1]).then_inc(p_ready, 1)
                eng.activation(ske[:, :], sk[:, :], ACT.Exp).then_inc(ske_ready, 1)
                for c in range(2):
                    eng.wait_ge(pT_psum, 2 * t + c + 1)
                    src = (2, 6)[c]
                    eng.copy(pT[:, c, :, :].rearrange("p h t -> p (h t)"), psum[:, src * BANK:(src + 2) * BANK])\
                       .then_inc(pT_ready, 1)
                eng.wait_ge(catT_psum, t + 1)
                eng.copy(catT[:, :, :].rearrange("p k t -> p (k t)"), psum[:, 4 * BANK:6 * BANK])\
                   .then_inc(catT_ready, 1)

            eng.dma_start(w_inv, WIN.rearrange("(k p) n -> p k n", p=P)).then_inc(weights_loaded, 16)
            eng.dma_start(w_out[:, :, :], WOUT.rearrange("(k p) n -> p k n", p=P)).then_inc(w_out_loaded, 16)
            eng.wait_ge(init_done, 3)
            with eng.Fori(0, PROMPT_TILES) as t:
                tile(t, False)
            tile(SAMPLE, True)

        @block.vector
        def _(eng):
            STEPS = 14

            def tile(t, sample):
                chain = Chain(eng, dve_step, STEPS * t)
                eng.wait_ge(std_ready, t + 1)
                chain.after(eng.reciprocal(rstd[:, :], std[:, :]))
                eng.scalar_tensor_tensor(out=h[:, :], in0=xt[:, :], scalar=rstd[:, 0:1], in1=gain[:, :],
                                         op0=ALU.mult, op1=ALU.mult).then_inc(h_ready, 1)
                eng.wait_ge(tab_loaded, 16 * t + 16)
                eng.wait_ge(zs_ready, 6 * t + 2)
                if sample:
                    eng.wait_ge(mode_loaded, 32)
                z16 = zs[:, 0:1024].rearrange("p (h e) -> p h e", e=HD)
                qk16 = qk[:, :].rearrange("p (h e) -> p h e", e=HD)
                rot16 = rot[:, :].rearrange("p (h e) -> p h e", e=HD)
                eng.wait_ge(x1_stored, 16 * t)
                eng.tensor_tensor(qk16, z16, spread(tab[:, T_C:T_C + HD], 1, 16), ALU.mult)
                eng.tensor_tensor(rot16[:, :, 0:32], z16[:, :, 32:64], spread(tab[:, T_S:T_S + 32], 1, 16), ALU.mult)
                chain.after(eng.tensor_tensor(rot16[:, :, 32:64], z16[:, :, 0:32],
                                              spread(tab[:, T_S + 32:T_S + 64], 1, 16), ALU.mult))
                eng.tensor_tensor(qk[:, :], qk[:, :], rot[:, :], ALU.add).then_inc(rot_ready, 1)
                eng.wait_ge(rot_ready, 2 * t + 1)
                eng.tensor_tensor(kd[:, :].rearrange("p (h e) -> p h e", e=HD), qk16[:, HEADS:, :],
                                  spread(mode[:, M_DK:M_DK + HEADS], 2, HD), ALU.mult).then_inc(rot_ready, 1)
                eng.wait_ge(zs_ready, 6 * t + 4)
                za = zs[:, Z_QA:Z_VA].rearrange("p (h e) -> p h e", e=HD)
                eng.tensor_tensor(rota[:, :, :], za[:, :, 0:16], spread(tab[:, T_CA:T_CA + 16], 1, 10), ALU.mult)
                eng.tensor_tensor(rotb[:, :, 0:8], za[:, :, 8:16], spread(tab[:, T_SA:T_SA + 8], 1, 10), ALU.mult)
                chain.after(eng.tensor_tensor(rotb[:, :, 8:16], za[:, :, 0:8],
                                              spread(tab[:, T_SA + 8:T_SA + 16], 1, 10), ALU.mult))
                eng.tensor_tensor(za[:, :, 0:16], rota[:, :, :], rotb[:, :, :], ALU.add).then_inc(rota_ready, 1)
                eng.wait_ge(rota_ready, 2 * t + 1)
                eng.tensor_copy(kad[:, :, :, :], spread(zs[:, Z_KA:Z_VA].rearrange("p (g e) -> p g e", g=KV), 2, 2))\
                   .then_inc(rota_ready, 1)
                eng.wait_ge(qkT_ready, 4 * t + 1)
                qd = eng.tensor_tensor(qTd[:, :, :].rearrange("p q t -> p (q t)"),
                                       qT[:, :, :].rearrange("p q t -> p (q t)"), mode[:, M_DQ:M_DK], ALU.mult)
                if not sample:
                    qd.then_inc(qTd_ready, 1)
                else:
                    qd.then_inc(qTd_ready, 1)
                    eng.wait_ge(qTd_ready, t + 1)
                    eng.wait_ge(zeroed, 7)
                    eng.wait_ge(qkT_ready, 4 * t + 3)
                    for dst, src in ((qaTm, qaT), (qTdm, qTd)):
                        for q in range(PAIRS):
                            own = bass.AP(dst.tensor, dst.offset + q * STREAMS * P,
                                          [dst.ap[0], [P + DEC, STREAMS], [1, DEC]])
                            last = eng.tensor_copy(own, src[:, q, :].rearrange("p (b i) -> p b i", i=DEC))
                        last.then_inc(masked_ready, 1)
                    eng.wait_ge(zs_ready, 6 * t + 5)
                    for hh in range(HEADS):
                        last = eng.tensor_tensor(vm[:, hh], spread(zs[:, Z_V + hh * HD:Z_V + (hh + 1) * HD], 1, STREAMS),
                                                 spread(bmask, 2, HD), ALU.mult)
                    last.then_inc(masked_ready, 1)
                eng.wait_ge(sc_psum, t + 1)
                eng.tensor_tensor(scT[:, :, :, :].rearrange("p r q t -> p (r q t)"), psum[:, 2 * BANK:4 * BANK],
                                  mode[:, M_MASK:M_DQ], ALU.mult).then_inc(scT_ready, 1)
                eng.wait_ge(sw_psum, t + 1)
                for r, b in ((0, 6), (1, 0)):
                    last = eng.scalar_tensor_tensor(
                        out=sm[:, 4 * r:4 * r + 4, :],
                        in0=psum[:, b * BANK:(b + 2) * BANK].rearrange("p (q s) -> p q s", q=PAIRS),
                        scalar=HD ** -0.5, in1=spread(tab[:, T_MASK:T_COLS], 1, PAIRS), op0=ALU.mult, op1=ALU.add)
                chain.after(last)
                chain.after(eng.tensor_reduce(mx[:, :], sm[:, :, :], AX.X, ALU.max))
                chain.after(eng.tensor_tensor(mx[:, :], mx[:, :], sinks[:, :], ALU.max))
                eng.tensor_tensor(sk[:, :], sinks[:, :], mx[:, :], ALU.subtract)
                eng.tensor_scalar(nmx[:, :], mx[:, :], -1.0, None, ALU.mult).then_inc(mx_ready, 1)
                if not sample:
                    eng.wait_ge(st_psum, t + 1)
                    eng.wait_ge(o_psum, t + 1)
                    for q in range(PAIRS):
                        for r in range(2):
                            s = slice(64 * r, 64 * r + 64)
                            at = 5 * BANK + q * P + r * HD
                            eng.scalar_tensor_tensor(out=S[s, q, s], in0=S[s, q, s], scalar=mode[s, M_G + q:M_G + q + 1],
                                                     in1=psum[s, at:at + HD], op0=ALU.mult, op1=ALU.add)\
                               .then_inc(S_ready, 1)
                else:
                    eng.wait_ge(o_psum, t + 1)
                    for hh in range(HEADS):
                        q, r = hh // 2, hh % 2
                        s = slice(64 * r, 64 * r + 64)
                        eng.wait_ge(st_psum, t + hh + 1)
                        dst = S0[s, q, :, s]
                        eng.scalar_tensor_tensor(out=dst, in0=dst, scalar=mode[s, M_G + q:M_G + q + 1],
                                                 in1=psum[s, 5 * BANK:6 * BANK].rearrange("p (b e) -> p b e", e=HD), op0=ALU.mult, op1=ALU.add)\
                           .then_inc(S_ready, 1)
                o8 = psum[:, 4 * BANK:5 * BANK].rearrange("p (h e) -> p h e", e=HD)
                dev8 = dev.rearrange("p (h e) -> p h e", e=HD)
                dsq8 = dsq.rearrange("p (h e) -> p h e", e=HD)
                chain.after(eng.tensor_reduce(gsum[:, :], o8, AX.X, ALU.add))
                chain.after(eng.scalar_tensor_tensor(out=dev8, in0=spread(gsum[:, :], 2, HD), scalar=-1.0 / HD,
                                                     in1=o8, op0=ALU.mult, op1=ALU.add))
                chain.after(eng.tensor_tensor(dsq, dev, dev, ALU.mult))
                eng.tensor_reduce(gvar[:, :], dsq8, AX.X, ALU.add).then_inc(gvar_ready, 1)
                eng.wait_ge(gstd_ready, t + 1)
                chain.after(eng.reciprocal(grstd[:, :], gstd[:, :]))
                chain.after(eng.tensor_tensor(dev8, dev8, spread(grstd[:, :], 2, HD), ALU.mult))
                eng.wait_ge(zs_ready, 6 * t + 6)
                chain.after(eng.tensor_tensor(cat[:, 0:512], dev, zs[:, Z_G:Z_QA], ALU.mult))
                eng.wait_ge(ske_ready, t + 1)
                chain.after(eng.tensor_tensor(den[:, :], den[:, :], ske[:, :], ALU.add))
                chain.after(eng.reciprocal(rden[:, :], den[:, :]))
                if sample:
                    for hh in range(HEADS):
                        i = (hh % 2) * PAIRS + hh // 2
                        if hh == 0:
                            eng.wait_ge(pT_ready, 2 * t + 2)
                        if hh >= 2:
                            eng.wait_ge(pTm_used, hh - 1)
                        own = bass.AP(pTm.tensor, pTm.offset + (hh % 2) * STREAMS * P,
                                      [pTm.ap[0], [P + DEC, STREAMS], [1, DEC]])
                        eng.tensor_copy(own, pT[:, 0, i, :].rearrange("p (b i) -> p b i", i=DEC))\
                           .then_inc(pTm_ready, 1)
                eng.wait_ge(oa_psum, t + 1)
                for r in range(2):
                    last = eng.tensor_tensor(
                        cat[:, 512:1024].rearrange("p (q r e) -> p q r e", r=2, e=HD)[:, :, r, :],
                        psum[:, 0:BANK].rearrange("p (q r e) -> p q r e", r=2, e=HD)[:, :, r, :],
                        spread(rden[:, 4 * r:4 * r + 4], 2, HD), ALU.mult)
                last.then_inc(cat_ready, 1)
                if not sample:
                    eng.tensor_copy(kaT[:, :, 0, :], kaT[:, :, 1, :])
                    eng.tensor_copy(v_prev[:, :], zs[:, Z_VA:IN_W]).then_inc(shifted, 1)
                eng.wait_ge(y_psum, t + 1)
                eng.tensor_tensor(x1t[:, :], xt[:, :], psum[:, 2 * BANK:4 * BANK], ALU.add).then_inc(x1_ready, 1)
                assert chain.n == STEPS, chain.n

            eng.wait_ge(const_loaded, 32)
            eng.wait_ge(mode_loaded, 16)
            eng.wait_ge(init_done, 3)
            with eng.Fori(0, PROMPT_TILES) as t:
                tile(t, False)
            tile(SAMPLE, True)


class SearchChain(Chain):

    def __init__(self, eng, sem, base, column):
        super().__init__(eng, sem, base)
        self.column = column

    def hold(self):
        self.eng.tensor_copy(self.column[:, 0:1], self.column[:, 1:2])

    def after(self, ins):
        super().after(ins)
        self.hold()


def top16(eng, chain, values, spare, best, where, groups):
    for g in range(groups):
        last = eng.max(best[:, g, 0:8], values[:, g, :])
    chain.after(last)
    for g in range(groups):
        eng.max_index(where[:, g, 0:8], best[:, g, 0:8], values[:, g, :])
        last = eng.match_replace(spare[:, g, :], best[:, g, 0:8], values[:, g, :], LOWEST)
    chain.after(last)
    for g in range(groups):
        last = eng.max(best[:, g, 8:16], spare[:, g, :])
    chain.after(last)
    for g in range(groups):
        last = eng.max_index(where[:, g, 8:16], best[:, g, 8:16], spare[:, g, :])
    chain.after(last)


def stage_route(nc, psum, dr, chosenT):
    with ExitStack() as ctx:
        def sb(name, shape, dt=F32):
            return ctx.enter_context(nc.sbuf_tensor("r_" + name, shape, dt))

        def sem(name):
            return ctx.enter_context(nc.semaphore("r_" + name))

        w_q = sb("w_q", [P, KC, SIDES * P])
        keys = sb("keys", [P, SIDES, NKEYS])
        gain = sb("gain", [P, D])
        ident = sb("ident", [P, P])
        xt = sb("xt", [P, D])
        h = sb("h", [P, D])
        hT = sb("hT", [P, KC, P])
        qT = sb("qT", [P, SIDES, P])
        s = sb("s", [P, SIDES, NKEYS])
        spare = sb("spare", [P, SIDES * NKEYS])
        cand = sb("cand", [P, PEER_HEADS, TOPK * TOPK])
        best = sb("best", [P, SIDES, TOPK])
        where = sb("where", [P, SIDES, TOPK], U32)
        wheref = sb("wheref", [P, SIDES, TOPK])
        sc = sb("sc", [P, PEER_HEADS, TOPK])
        sel = sb("sel", [P, PEER_HEADS, TOPK], U32)
        rank = sb("rank", [P, 2, CHOSEN], U32)
        rankf = sb("rankf", [P, 2, CHOSEN])
        iota = sb("iota", [P, TOPK])
        eq = sb("eq", [P, CHOSEN, TOPK])
        chosen = sb("chosen", [P, 3, CHOSEN])
        e = sb("e", [P, PEER_HEADS, TOPK])
        esum = sb("esum", [P, PEER_HEADS])
        ss = sb("ss", [P, 1])
        std = sb("std", [P, 1])
        rstd = sb("rstd", [P, 1])
        held = sb("held", [P, 2])

        w_loaded = sem("w_loaded")
        gain_loaded = sem("gain_loaded")
        made = sem("made")
        held_made = sem("held_made")
        x_loaded = sem("x_loaded")
        act_step = sem("act_step")
        dve_step = sem("dve_step")
        std_ready = sem("std_ready")
        h_ready = sem("h_ready")
        hT_psum = sem("hT_psum")
        hT_ready = sem("hT_ready")
        hT_stored = sem("hT_stored")
        q_psum = sem("q_psum")
        qT_ready = sem("qT_ready")
        s_psum = sem("s_psum")
        s_ready = sem("s_ready")
        s_used = sem("s_used")
        sc_ready = sem("sc_ready")
        e_ready = sem("e_ready")
        chosen_ready = sem("chosen_ready")
        chosen_psum = sem("chosen_psum")
        chosenT_ready = sem("chosenT_ready")

        block = ctx.enter_context(nc.Block())

        @block.gpsimd
        def _(eng):
            eng.memset(ident[:, :], 0.0).then_inc(made, 1)
            eng.wait_ge(made, 1)
            eng.affine_select(out=ident[:, :], in_=ident[:, :], compare_op=ALU.not_equal, fill=1.0, base=0,
                              pattern=[[-1, P]], channel_multiplier=1).then_inc(made, 1)
            eng.iota(iota[:, :], pattern=[[1, TOPK]], base=0, channel_multiplier=0,
                     allow_small_or_imprecise_dtypes=True).then_inc(made, 1)

        @block.sync
        def _(eng):
            def load(t):
                eng.dma_start(xt[:, :], dr["x1"][t]).then_inc(x_loaded, 16)

            eng.dma_start(gain[:, :], dr["norm_ffn"].partition_broadcast(P)).then_inc(gain_loaded, 16)
            load(0)
            with eng.Fori(0, TILES - 1) as t:
                eng.wait_ge(h_ready, t + 1)
                load(t + 1)
                eng.wait_ge(hT_ready, t + 1)
                eng.dma_start(dr["h2T"][t], hT[:, :, :]).then_inc(hT_stored, 16)
            eng.wait_ge(hT_ready, TILES)
            eng.dma_start(dr["h2T"][TILES - 1], hT[:, :, :]).then_inc(hT_stored, 16)
            eng.wait_ge(hT_stored, 16 * TILES)

        @block.tensor
        def _(eng):
            def front(t, first=False):
                eng.wait_ge(h_ready, t + 1)
                eng.wait_ge(s_ready, t * 4)
                for k in range(KC):
                    mm = eng.transpose(psum[:, k * P:(k + 1) * P], h[:, k * P:(k + 1) * P], ident[:, :])
                mm.then_inc(hT_psum, 1)
                eng.wait_ge(hT_ready, t + 1)
                if not first:
                    eng.wait_ge(chosenT_ready, t - 1)
                for g in range(4):
                    for i in range(4):
                        at = 4 * g + i
                        out = psum[:, (2 + g) * BANK + i * P:(2 + g) * BANK + (i + 1) * P]
                        for k in range(KC):
                            mm = eng.matmul(out, w_q[:, k, at * P:(at + 1) * P], hT[:, k, :],
                                            start=(k == 0), stop=(k == KC - 1))
                    mm.then_inc(q_psum, 1)
                for g in range(4):
                    eng.wait_ge(qT_ready, 4 * t + g + 1)
                    for i in range(4):
                        at = 4 * g + i
                        b = (6, 7, 0, 1)[g]
                        mm = eng.matmul(psum[:, b * BANK + i * P:b * BANK + (i + 1) * P], qT[:, at, :],
                                        keys[:, at, :], start=True, stop=True)
                    mm.then_inc(s_psum, 1)

            def back(t):
                eng.wait_ge(chosen_ready, t + 1)
                for c in range(3):
                    mm = eng.transpose(psum[:, 2 * BANK + c * P:2 * BANK + (c + 1) * P], chosen[:, c, :], ident[:, :])
                mm.then_inc(chosen_psum, 1)

            eng.wait_ge(made, 3)
            eng.wait_ge(w_loaded, 32)
            front(0, True)
            with eng.Fori(1, TILES) as t:
                front(t)
                back(t - 1)
            back(TILES - 1)

        @block.scalar
        def _(eng):
            def front(t):
                chain = Chain(eng, act_step, t)
                eng.wait_ge(x_loaded, 16 * t + 16)
                chain.after(eng.activation(qT[:, 0:KC, :].rearrange("p k t -> p (k t)"), xt[:, :], ACT.Square,
                                           accum_out=ss[:, :]))
                eng.activation(std[:, :], ss[:, :], ACT.Sqrt, bias=EPS, scale=1.0 / D).then_inc(std_ready, 1)
                eng.wait_ge(hT_psum, t + 1)
                eng.wait_ge(hT_stored, 16 * t)
                eng.copy(hT[:, :, :].rearrange("p k t -> p (k t)"), psum[:, 0:2 * BANK]).then_inc(hT_ready, 1)
                for g in range(4):
                    eng.wait_ge(q_psum, 4 * t + g + 1)
                    eng.copy(qT[:, 4 * g:4 * g + 4, :].rearrange("p s t -> p (s t)"),
                             psum[:, (2 + g) * BANK:(3 + g) * BANK]).then_inc(qT_ready, 1)
                eng.wait_ge(s_used, t)
                for g in range(4):
                    b = (6, 7, 0, 1)[g]
                    eng.wait_ge(s_psum, 4 * t + g + 1)
                    eng.copy(s[:, 4 * g:4 * g + 4, :].rearrange("p s t -> p (s t)"),
                             psum[:, b * BANK:(b + 1) * BANK]).then_inc(s_ready, 1)

            def back(t):
                eng.wait_ge(sc_ready, t + 1)
                eng.activation(e[:, :, :], e[:, :, :], ACT.Exp).then_inc(e_ready, 1)
                eng.wait_ge(chosen_psum, t + 1)
                eng.copy(chosenT[:, :, bass.ds(t * P, P)],
                         psum[:, 2 * BANK:2 * BANK + 3 * P].rearrange("p (c t) -> p c t", c=3))\
                   .then_inc(chosenT_ready, 1)

            eng.dma_start(w_q[:, :, :], dr["w_q"].rearrange("(k p) n -> p k n", p=P)).then_inc(w_loaded, 16)
            eng.dma_start(keys[:, :, :], dr["keysT"]).then_inc(w_loaded, 16)
            front(0)
            with eng.Fori(1, TILES) as t:
                front(t)
                back(t - 1)
            back(TILES - 1)

        @block.vector
        def _(eng):
            STEPS = 20

            def front(t, base):
                eng.wait_ge(std_ready, t + 1)
                Chain(eng, dve_step, base).after(eng.reciprocal(rstd[:, :], std[:, :]))
                eng.scalar_tensor_tensor(out=h[:, :], in0=xt[:, :], scalar=rstd[:, 0:1], in1=gain[:, :],
                                         op0=ALU.mult, op1=ALU.mult).then_inc(h_ready, 1)

            def back(t, base):
                search = SearchChain(eng, dve_step, base, held)
                eng.wait_ge(s_ready, 4 * t + 4)
                search.hold()
                top16(eng, search, s[:, :, :], spare[:, :].rearrange("p (g n) -> p g n", g=SIDES),
                      best[:, :, :], where[:, :, :], SIDES)
                pair = best[:, :, :].rearrange("p (h c) r -> p h c r", c=2)
                cand4 = cand[:, :, :].rearrange("p h (a b) -> p h a b", a=TOPK)
                eng.tensor_copy(wheref[:, :, :], where[:, :, :]).then_inc(s_used, 1)
                search.after(eng.tensor_tensor(cand4, spread(pair[:, :, 0, :], 3, TOPK),
                                              spread(pair[:, :, 1, :], 2, TOPK), ALU.add))
                top16(eng, search, cand[:, :, :], spare[:, :].rearrange("p (g n) -> p g n", g=PEER_HEADS),
                      sc[:, :, :], sel[:, :, :], PEER_HEADS)
                chain = Chain(eng, dve_step, base + search.n)
                eng.tensor_tensor(e[:, :, :], sc[:, :, :], sc[:, :, 0:1].to_broadcast([P, PEER_HEADS, TOPK]),
                                  ALU.subtract).then_inc(sc_ready, 1)
                sel1 = sel[:, :, :].rearrange("p h k -> p (h k)")
                eng.tensor_scalar(rank[:, 0, :], sel1, 4, None, ALU.logical_shift_right)
                chain.after(eng.tensor_scalar(rank[:, 1, :], sel1, TOPK - 1, None, ALU.bitwise_and))
                chain.after(eng.tensor_copy(rankf[:, :, :], rank[:, :, :]))
                sides = wheref[:, :, :].rearrange("p (h c) r -> p h c r", c=2)
                eq4 = eq[:, :, :].rearrange("p (h k) r -> p h k r", h=PEER_HEADS)
                eng.wait_ge(chosen_psum, t)
                for c in range(2):
                    chain.after(eng.tensor_tensor(eq[:, :, :], spread(rankf[:, c, :], 2, TOPK),
                                                  spread(iota[:, :], 1, CHOSEN), ALU.is_equal))
                    chain.after(eng.tensor_tensor(eq4, eq4, spread(sides[:, :, c, :], 2, TOPK), ALU.mult))
                    chain.after(eng.tensor_reduce(chosen[:, c, :], eq[:, :, :], AX.X, ALU.add))
                eng.wait_ge(e_ready, t + 1)
                chain.after(eng.tensor_reduce(esum[:, :], e[:, :, :], AX.X, ALU.add))
                chain.after(eng.reciprocal(esum[:, :], esum[:, :]))
                eng.tensor_tensor(chosen[:, 2, :].rearrange("p (h k) -> p h k", h=PEER_HEADS), e[:, :, :],
                                  spread(esum[:, :], 2, TOPK), ALU.mult).then_inc(chosen_ready, 1)
                assert search.n + chain.n == STEPS - 1

            eng.wait_ge(gain_loaded, 16)
            eng.wait_ge(made, 3)
            eng.memset(held[:, :], 0.0).then_inc(held_made, 1)
            eng.wait_ge(held_made, 1)
            front(0, 0)
            with eng.Fori(1, TILES) as t:
                front(t, STEPS * (t - 1) + 1)
                back(t - 1, STEPS * (t - 1) + 2)
            back(TILES - 1, STEPS * (TILES - 1) + 1)


def stage_gates(nc, psum, dr, chosenT):
    GROUP = 8
    with ExitStack() as ctx:
        def sb(name, shape, dt=F32):
            return ctx.enter_context(nc.sbuf_tensor("g_" + name, shape, dt))

        def sem(name):
            return ctx.enter_context(nc.semaphore("g_" + name))

        iota = sb("iota", [P, P])
        gate_hi = sb("gate_hi", [P, TOKENS], F32R)
        gate_lo = sb("gate_lo", [P, TOKENS])
        rows_hi = [sb(f"rows_hi{i}", [P, GROUP, P], F32R) for i in range(2)]
        rows_lo = [sb(f"rows_lo{i}", [P, GROUP, P], F32R) for i in range(2)]
        cols = [sb(f"cols{i}", [P, GROUP, P], F32R) for i in range(2)]
        grid = sb("grid", [P, 2, NKEYS, P])

        made = sem("made")
        parts = sem("parts")
        onehot_ready = sem("onehot_ready")
        grid_psum = sem("grid_psum")
        grid_ready = sem("grid_ready")
        grid_stored = [sem(f"grid_stored{i}") for i in range(2)]
        GROUPS = P // GROUP

        block = ctx.enter_context(nc.Block())

        @block.gpsimd
        def _(eng):
            eng.iota(iota[:, :], pattern=[[1, P]], base=0, channel_multiplier=0,
                     allow_small_or_imprecise_dtypes=True).then_inc(made, 1)

        @block.vector
        def _(eng):
            eng.wait_ge(made, 1)
            eng.tensor_copy(gate_hi[:, :], chosenT[:, 2, :]).then_inc(parts, 1)
            eng.wait_ge(parts, 1)
            eng.tensor_tensor(gate_lo[:, :], chosenT[:, 2, :], gate_hi[:, :].bitcast(F32), ALU.subtract)\
               .then_inc(parts, 1)
            eng.wait_ge(parts, 2)

            def group(g, i, first):
                if not first:
                    eng.wait_ge(grid_psum, g - 1)
                for n in range(GROUP):
                    at = g * GROUP + n
                    row = chosenT[:, 0, bass.ds(at, 1)]
                    eng.tensor_scalar(rows_hi[i][:, n, :], iota[:, :], row, gate_hi[:, bass.ds(at, 1)].bitcast(F32),
                                      ALU.is_equal, ALU.mult)
                    eng.tensor_scalar(rows_lo[i][:, n, :], iota[:, :], row, gate_lo[:, bass.ds(at, 1)],
                                      ALU.is_equal, ALU.mult)
                    last = eng.tensor_scalar(cols[i][:, n, :], iota[:, :], chosenT[:, 1, bass.ds(at, 1)], None,
                                             ALU.is_equal)
                last.then_inc(onehot_ready, 1)

            group(0, 0, True)
            group(1, 1, True)
            with eng.Fori(1, TILES * GROUPS // 2) as m:
                group(m * 2, 0, False)
                group(m * 2 + 1, 1, False)

        @block.tensor
        def _(eng):
            def group(g, i, first):
                eng.wait_ge(onehot_ready, g + 1)
                if not first:
                    eng.wait_ge(grid_ready, g - 1)
                for n in range(GROUP):
                    out = psum[:, 2 * i * BANK + n * P:2 * i * BANK + (n + 1) * P]
                    eng.matmul(out, rows_lo[i][:, n, :], cols[i][:, n, :], start=True, stop=False)
                    mm = eng.matmul(out, rows_hi[i][:, n, :], cols[i][:, n, :], start=False, stop=True)
                mm.then_inc(grid_psum, 1)

            group(0, 0, True)
            group(1, 1, True)
            with eng.Fori(1, TILES * GROUPS // 2) as m:
                group(m * 2, 0, False)
                group(m * 2 + 1, 1, False)

        @block.scalar
        def _(eng):
            def group(t, g, i, slot):
                eng.wait_ge(grid_psum, t * GROUPS + g + 1)
                eng.copy(grid[:, slot, :, bass.ds(g * GROUP, GROUP)],
                         psum[:, 2 * i * BANK:(2 * i + 2) * BANK].rearrange("p (t j) -> p j t", t=GROUP))\
                   .then_inc(grid_ready, 1)

            def tile(t, slot):
                with eng.Fori(0, GROUPS // 2) as m:
                    group(t, m * 2, 0, slot)
                    group(t, m * 2 + 1, 1, slot)

            tile(0, 0)
            tile(1, 1)
            with eng.Fori(1, TILES // 2) as n:
                for slot in range(2):
                    eng.wait_ge(grid_stored[slot], 16 * n)
                    tile(n * 2 + slot, slot)
            eng.wait_ge(grid_stored[0], 16 * (TILES // 2))
            tile(TILES - 1, 0)

        @block.sync
        def _(eng):
            def store(t, slot):
                eng.wait_ge(grid_ready, GROUPS * t + GROUPS)
                eng.dma_start(dr["gates"][t], grid[:, slot, :, :]).then_inc(grid_stored[slot], 16)

            with eng.Fori(0, TILES // 2) as n:
                store(n * 2, 0)
                store(n * 2 + 1, 1)
            store(TILES - 1, 0)
            eng.wait_ge(grid_stored[0], 16 * (TILES // 2 + 1))
            eng.wait_ge(grid_stored[1], 16 * (TILES // 2))


def stage_experts(nc, psum, dr):
    COLS = NKEYS
    with ExitStack() as ctx:
        def sb(name, shape, dt=F32):
            return ctx.enter_context(nc.sbuf_tensor("e_" + name, shape, dt))

        def sem(name):
            return ctx.enter_context(nc.semaphore("e_" + name))

        gain = sb("gain", [P, D])
        h_raw = sb("h_raw", [P, BT, KC, P])
        h_hi = sb("h_hi", [P, KC, BT, P], F32R)
        h_lo = sb("h_lo", [P, KC, BT, P], F32R)
        u_raw = [sb(f"u_raw{i}", [P, 2, D]) for i in range(2)]
        v_raw = [sb(f"v_raw{i}", [P, 2, D]) for i in range(2)]
        g_raw = [sb(f"g_raw{i}", [P, BT, 2, P]) for i in range(2)]
        u_hi = [sb(f"u_hi{i}", [P, D], F32R) for i in range(2)]
        u_lo = [sb(f"u_lo{i}", [P, D], F32R) for i in range(2)]
        v_hi = [sb(f"v_hi{i}", [P, D], F32R) for i in range(2)]
        v_lo = [sb(f"v_lo{i}", [P, D], F32R) for i in range(2)]
        gl = [sb(f"gl{i}", [P, BTOK]) for i in range(2)]
        a = [sb(f"a{i}", [P, BTOK]) for i in range(2)]
        a_hi = [sb(f"a_hi{i}", [P, BTOK], F32R) for i in range(2)]
        a_lo = [sb(f"a_lo{i}", [P, BTOK], F32R) for i in range(2)]
        x1 = sb("x1", [P, BT, D])
        sq = sb("sq", [P, BT, D])
        y = sb("y", [P, BT, D])
        ss = sb("ss", [P, BT])
        std = sb("std", [P, BT])
        rstd = sb("rstd", [P, BT])

        gain_loaded = sem("gain_loaded")
        h_loaded = sem("h_loaded")
        h_hi_ready = sem("h_hi_ready")
        h_ready = sem("h_ready")
        u_loaded = [sem(f"u_loaded{i}") for i in range(2)]
        v_loaded = [sem(f"v_loaded{i}") for i in range(2)]
        g_loaded = [sem(f"g_loaded{i}") for i in range(2)]
        u_hi_ready = sem("u_hi_ready")
        u_ready = sem("u_ready")
        v_hi_ready = sem("v_hi_ready")
        v_ready = sem("v_ready")
        s_done = sem("s_done")
        gl_ready = sem("gl_ready")
        dve_step = sem("dve_step")
        a_ready = sem("a_ready")
        o_done = sem("o_done")
        x1_loaded = sem("x1_loaded")
        sum_ready = sem("sum_ready")
        ss_ready = sem("ss_ready")
        std_ready = sem("std_ready")
        y_ready = sem("y_ready")
        y_stored = sem("y_stored")

        UNROLL = 4
        TURNS = COLS // UNROLL

        def each_column(eng, step):
            for i in range(UNROLL):
                step(0, i, i == 0, False)
            with eng.Fori(1, TURNS - 1) as n:
                for i in range(UNROLL):
                    step(n, i, False, False)
            for i in range(UNROLL):
                step(TURNS - 1, i, False, UNROLL - i)

        block = ctx.enter_context(nc.Block())

        @block.sync
        def _(eng):
            def pair(b, n, slot, first):
                at = n * 4 + 2 * slot
                done = b * COLS + n * 4 + 2 * slot - 2
                src_g = dr["gates"][bass.ds(b * BT, BT), :, bass.ds(at, 2), :].rearrange("t p j q -> p t j q")
                src_u = dr["uT"][bass.ds(at, 2)].rearrange("j p n -> p j n")
                src_v = dr["v"][:, bass.ds(at, 2), :]
                if not first:
                    eng.wait_ge(u_ready, done)
                eng.dma_start(u_raw[slot][:, :, :], src_u).then_inc(u_loaded[slot], 16)
                if not first:
                    eng.wait_ge(v_ready, done)
                eng.dma_start(v_raw[slot][:, :, :], src_v).then_inc(v_loaded[slot], 16)
                if not first:
                    eng.wait_ge(a_ready, done)
                eng.dma_start(g_raw[slot][:, :, :, :], src_g).then_inc(g_loaded[slot], 16)

            def h_in(b):
                src = dr["h2T"][bass.ds(b * BT, BT)].rearrange("t p n -> p t n")
                eng.wait_ge(h_ready, b)
                eng.dma_start(h_raw[:, :, :, :].rearrange("p t k q -> p t (k q)"), src).then_inc(h_loaded, 16)

            def tail(b):
                src = dr["x1"][bass.ds(b * BT, BT)].rearrange("t p n -> p t n")
                dst = dr["y"][bass.ds(b * BT, BT)].rearrange("t p n -> p t n")
                eng.dma_start(x1[:, :, :], src).then_inc(x1_loaded, 16)
                eng.wait_ge(y_ready, BT * b + BT)
                eng.dma_start(dst, y[:, :, :]).then_inc(y_stored, 16)

            eng.dma_start(gain[:, :], dr["norm_final"].partition_broadcast(P)).then_inc(gain_loaded, 16)
            h_in(0)
            pair(0, 0, 0, True)
            pair(0, 0, 1, True)
            with eng.Fori(1, TURNS) as n:
                pair(0, n, 0, False)
                pair(0, n, 1, False)
            tail(0)
            with eng.Fori(1, BLOCKS) as b:
                h_in(b)
                with eng.Fori(0, TURNS) as n:
                    pair(b, n, 0, False)
                    pair(b, n, 1, False)
                tail(b)
            eng.wait_ge(y_stored, 16 * BLOCKS)

        @block.tensor
        def _(eng):
            def scores(at, i):
                out = psum[:, (6 + i % 2) * BANK:(6 + i % 2) * BANK + BTOK]
                eng.wait_ge(u_ready, at + 1)
                n = 0
                for w, x in ((u_lo, h_hi), (u_hi, h_lo), (u_hi, h_hi)):
                    for k in range(KC):
                        mm = eng.matmul(out, w[i % 2][:, k * P:(k + 1) * P],
                                        x[:, k, :, :].rearrange("p t q -> p (t q)"),
                                        start=(n == 0), stop=(n == 3 * KC - 1))
                        n += 1
                mm.then_inc(s_done, 1)

            def outputs(at, i, first, last):
                eng.wait_ge(a_ready, at + 1)
                eng.wait_ge(v_ready, at + 1)
                i %= 2
                for t in range(BT):
                    for n, (x, w) in enumerate(((a_lo, v_hi), (a_hi, v_lo), (a_hi, v_hi))):
                        for half in range(2):
                            mm = eng.matmul(psum[:, (2 * t + half) * BANK:(2 * t + half + 1) * BANK],
                                            x[i][:, t * P:(t + 1) * P], w[i][:, half * BANK:(half + 1) * BANK],
                                            start=(first and n == 0), stop=(last and n == 2))
                mm.then_inc(o_done, 1)

            with eng.Fori(0, BLOCKS) as b:
                def step(n, i, first, left):
                    at = b * COLS + n * UNROLL + i
                    if left != 1:
                        if not first:
                            eng.wait_ge(gl_ready, at)
                        scores(at + 1, i + 1)
                    if first:
                        eng.wait_ge(sum_ready, BT * b)
                    outputs(at, i, first, left == 1)

                eng.wait_ge(h_ready, b + 1)
                scores(b * COLS, 0)
                each_column(eng, step)

        @block.scalar
        def _(eng):
            def split_u(b, n, i):
                if i % 2 == 0:
                    eng.wait_ge(u_loaded[i // 2], (b * TURNS + n + 1) * 16)
                eng.copy(u_hi[i % 2][:, :], u_raw[i // 2][:, i % 2, :]).then_inc(u_hi_ready, 1)

            def split_v(b, n, i):
                if i % 2 == 0:
                    eng.wait_ge(v_loaded[i // 2], (b * TURNS + n + 1) * 16)
                eng.copy(v_hi[i % 2][:, :], v_raw[i // 2][:, i % 2, :]).then_inc(v_hi_ready, 1)

            with eng.Fori(0, BLOCKS) as b:
                def step(n, i, first, left):
                    at = b * COLS + n * UNROLL + i
                    eng.wait_ge(s_done, at + 1)
                    eng.activation(gl[i % 2][:, :], psum[:, (6 + i % 2) * BANK:(6 + i % 2) * BANK + BTOK],
                                   ACT.Gelu_apprx_tanh).then_inc(gl_ready, 1)
                    if left not in (1, 2):
                        split_u(b, n + (i + 2) // 4, (i + 2) % 4)
                    if left != 1:
                        eng.wait_ge(o_done, at)
                        split_v(b, n + (i + 1) // 4, (i + 1) % 4)

                eng.wait_ge(h_loaded, 16 * b + 16)
                eng.wait_ge(o_done, b * COLS)
                eng.copy(h_hi[:, :, :, :], h_raw[:, :, :, :].rearrange("p t k q -> p k t q")).then_inc(h_hi_ready, 1)
                split_u(b, 0, 0)
                split_u(b, 0, 1)
                split_v(b, 0, 0)
                each_column(eng, step)
                for t in range(BT):
                    eng.wait_ge(sum_ready, BT * b + t + 1)
                    eng.activation(sq[:, t, :], y[:, t, :], ACT.Square, accum_out=ss[:, t:t + 1]).then_inc(ss_ready, 1)
                eng.wait_ge(ss_ready, BT * b + BT)
                eng.activation(std[:, :], ss[:, :], ACT.Sqrt, bias=EPS, scale=1.0 / D).then_inc(std_ready, 1)

        @block.vector
        def _(eng):
            def split_u(at, i):
                eng.wait_ge(u_hi_ready, at + 1)
                eng.tensor_tensor(u_lo[i % 2][:, :], u_raw[i // 2][:, i % 2, :], u_hi[i % 2][:, :].bitcast(F32),
                                  ALU.subtract).then_inc(u_ready, 1)

            def split_v(at, i):
                eng.wait_ge(v_hi_ready, at + 1)
                eng.tensor_tensor(v_lo[i % 2][:, :], v_raw[i // 2][:, i % 2, :], v_hi[i % 2][:, :].bitcast(F32),
                                  ALU.subtract).then_inc(v_ready, 1)

            eng.wait_ge(gain_loaded, 16)
            with eng.Fori(0, BLOCKS) as b:
                def step(n, i, first, left):
                    at = b * COLS + n * UNROLL + i
                    if i % 2 == 0:
                        eng.wait_ge(g_loaded[i // 2], (b * TURNS + n + 1) * 16)
                    eng.wait_ge(gl_ready, at + 1)
                    eng.tensor_tensor(a[i % 2][:, :].rearrange("p (t q) -> p t q", t=BT),
                                      gl[i % 2][:, :].rearrange("p (t q) -> p t q", t=BT),
                                      g_raw[i // 2][:, :, i % 2, :], ALU.mult).then_inc(dve_step, 1)
                    eng.wait_ge(dve_step, 2 * at + b + 1)
                    eng.tensor_copy(a_hi[i % 2][:, :], a[i % 2][:, :]).then_inc(dve_step, 1)
                    eng.wait_ge(dve_step, 2 * at + b + 2)
                    eng.tensor_tensor(a_lo[i % 2][:, :], a[i % 2][:, :], a_hi[i % 2][:, :].bitcast(F32),
                                      ALU.subtract).then_inc(a_ready, 1)
                    if left not in (1, 2):
                        split_u(at + 2, (i + 2) % 4)
                    if left != 1:
                        split_v(at + 1, (i + 1) % 4)

                eng.wait_ge(h_hi_ready, b + 1)
                eng.tensor_tensor(h_lo[:, :, :, :], h_raw[:, :, :, :].rearrange("p t k q -> p k t q"),
                                  h_hi[:, :, :, :].bitcast(F32), ALU.subtract).then_inc(h_ready, 1)
                split_u(b * COLS, 0)
                split_u(b * COLS + 1, 1)
                split_v(b * COLS, 0)
                each_column(eng, step)
                eng.wait_ge(o_done, b * COLS + COLS)
                eng.wait_ge(x1_loaded, 16 * b + 16)
                eng.wait_ge(y_stored, 16 * b)
                for t in range(BT):
                    eng.tensor_tensor(y[:, t, :], x1[:, t, :], psum[:, 2 * t * BANK:(2 * t + 2) * BANK], ALU.add)\
                       .then_inc(sum_ready, 1)
                eng.wait_ge(std_ready, b + 1)
                eng.reciprocal(rstd[:, :], std[:, :]).then_inc(dve_step, 1)
                eng.wait_ge(dve_step, 2 * COLS * (b + 1) + b + 1)
                for t in range(BT):
                    eng.scalar_tensor_tensor(out=y[:, t, :], in0=y[:, t, :], scalar=rstd[:, t:t + 1], in1=gain[:, :],
                                             op0=ALU.mult, op1=ALU.mult).then_inc(y_ready, 1)


def program(nc, dr, stages="mrge"):
    with ExitStack() as ctx:
        psum = ctx.enter_context(nc.psum_tensor("psum", [P, 8 * BANK], F32))[:, :]
        if "m" in stages:
            stage_mix(nc, psum, dr)
        if "r" in stages:
            chosenT = ctx.enter_context(nc.sbuf_tensor("chosenT_sb", [P, 3, TOKENS], F32))[:, :, :]
            stage_route(nc, psum, dr, chosenT)
            if "chosenT" in dr:
                with nc.semaphore("dbg") as dbg, nc.Block() as block:
                    @block.sync
                    def _(eng):
                        eng.dma_start(dr["chosenT"], chosenT).then_inc(dbg, 16)
                        eng.wait_ge(dbg, 16)
        if "g" in stages:
            stage_gates(nc, psum, dr, chosenT)
        if "e" in stages:
            stage_experts(nc, psum, dr)


def host_inputs(inp):
    c = np.ascontiguousarray
    state = inp["state_ret"][0].reshape(STREAMS, PAIRS, 2, HD, HD)
    kc = inp["cache_swa_k"][0]
    return {
        "x": np.concatenate([inp["x_prompt"].reshape(-1, D), inp["x_sample"].reshape(-1, D)]).reshape(TILES, P, D),
        "tile_tab": tile_tables(),
        "mode_tab": mode_tables(),
        "norm_mix": c(inp["norm_mix"][0]),
        "norm_ffn": c(inp["norm_ffn"][0]),
        "norm_final": c(inp["norm_final"]),
        "sinks": c(inp["attn_sinks"][0].reshape(PAIRS, 2).T.reshape(HEADS)),
        "w_in": c(inp["w_in"][0]),
        "w_out": c(inp["w_out"][0]),
        "w_q": c(inp["peer_w_q"][0]),
        "keysT": c(inp["peer_keys"][0].reshape(SIDES, NKEYS, P).transpose(2, 0, 1)),
        "uT": c(inp["peer_u"][0].reshape(NKEYS, NKEYS, KC, P).transpose(1, 3, 2, 0).reshape(NKEYS, P, D)),
        "v": inp["peer_v"][0].reshape(NKEYS, NKEYS, D),
        "s0": c(state.transpose(2, 3, 1, 0, 4)),
        "kcT": c(kc.transpose(3, 2, 0, 1)),
        "kc": c(kc.reshape(STREAMS, WINDOW, KV * HD)),
        "vc": c(inp["cache_swa_v"][0].reshape(STREAMS, WINDOW, KV * HD)),
    }


OUTPUTS = {
    "y": (TILES, P, D),
    "o_sp": (HEADS, HD, HD),
    "o_kp": (P, P),
    "o_vp": (P, P),
    "o_ss": (2, HD, PAIRS, STREAMS, HD),
    "o_ks": (STREAMS, WINDOW, P),
    "o_vs": (STREAMS, WINDOW, P),
}
SCRATCH = {
    "x1": (TILES, P, D),
    "h2T": (TILES, P, D),
    "gates": (TILES, P, NKEYS, P),
}


def build(nc, arrays, stages="mrge", show=()):
    dr = {}
    for name, a in arrays.items():
        dr[name] = nc.dram_tensor(name, a.shape, mybir.dt.from_np(a.dtype), kind="ExternalInput").ap()
    for name, shape in OUTPUTS.items():
        dr[name] = nc.dram_tensor(name, shape, F32, kind="ExternalOutput").ap()
    for name, shape in SCRATCH.items():
        dr[name] = nc.dram_tensor(name, shape, F32, kind="ExternalOutput" if name in show else "Internal").ap()
    if "chosenT" in show:
        dr["chosenT"] = nc.dram_tensor("chosenT", (P, 3, TOKENS), F32, kind="ExternalOutput").ap()
    program(nc, dr, stages)


def kernel(**inputs):
    import concourse.bacc as bacc
    from concourse.bass_utils import run_bass_kernel_spmd

    arrays = host_inputs({k: np.asarray(v) for k, v in inputs.items()})
    nc = bacc.Bacc("TRN2", target_bir_lowering=False, num_devices=1)
    build(nc, arrays)
    r = run_bass_kernel_spmd(nc, [arrays], core_ids=[0]).results[0]
    y = r["y"].reshape(TOKENS, D)
    state = r["o_ss"].transpose(3, 2, 0, 1, 4).reshape(1, STREAMS, HEADS, HD, HD)
    return (
        y[:SEQ].reshape(1, SEQ, D),
        y[SEQ:].reshape(STREAMS, DEC, D),
        r["o_sp"].reshape(1, 1, HEADS, HD, HD),
        r["o_kp"].reshape(1, 1, WINDOW, KV, HD),
        r["o_vp"].reshape(1, 1, WINDOW, KV, HD),
        np.ascontiguousarray(state),
        r["o_ks"].reshape(1, STREAMS, WINDOW, KV, HD),
        r["o_vs"].reshape(1, STREAMS, WINDOW, KV, HD),
    )
```

```python
from contextlib import ExitStack

import numpy as np

import concourse.bass as bass
from concourse import mybir

F32 = mybir.dt.float32
F32R = mybir.dt.float32r
BF16 = mybir.dt.bfloat16
U32 = mybir.dt.uint32
ALU = mybir.AluOpType
ACT = mybir.ActivationFunctionType
AX = mybir.AxisListType

P = 128
D = 1024
KC = D // P
SEQ = 1024
STREAMS = 8
DEC = 16
PAST = 512
PROMPT_TILES = SEQ // P
TILES = PROMPT_TILES + 1
SAMPLE = PROMPT_TILES
TOKENS = TILES * P
HEADS = 8
PAIRS = HEADS // 2
HD = 64
KV = 2
CHUNK = 64
WINDOW = 128
IN_W = 2816
EPS = 1e-6
RET_THETA = 10000.0
ROPE_THETA = 500000.0
ROPE_DIM = HD // 4
NEG = -1e30
LOWEST = -3.0e38

Z_Q, Z_K, Z_V, Z_G, Z_QA, Z_KA, Z_VA = 0, 512, 1024, 1536, 2048, 2560, 2688
BANK = 512

PEER_HEADS = 8
SIDES = 2 * PEER_HEADS
NKEYS = 128
TOPK = 16
CHOSEN = PEER_HEADS * TOPK
CAND_RECTS = ((0, 1, 16), (1, 3, 8), (4, 4, 4), (8, 8, 1))
CANDS = 64
START = (0, 16, 24, 32, 40, 44, 48, 52) + tuple(range(56, CANDS))
BLOCKS = 3
BT = TILES // BLOCKS
BTOK = BT * P
GATE_CHUNK = 64

T_C, T_S, T_CA, T_SA, T_MASK, T_COLS = 0, 64, 128, 144, 160, 416
M_MASK, M_DQ, M_DK, M_G, M_COLS = 0, 1024, 1536, 1544, 1548


def rope_tables(pos, rot, theta):
    half = rot // 2
    freqs = np.float32(theta) ** (-np.arange(half, dtype=np.float32) / np.float32(half))
    ang = pos[:, None] * freqs[None, :]
    c, s = np.cos(ang), np.sin(ang)
    return np.concatenate([c, c], 1), np.concatenate([-s, s], 1)


def tile_tables():
    pos = np.concatenate([np.arange(SEQ), PAST + np.arange(P) % DEC]).astype(np.float32)
    out = np.zeros((TILES, P, T_COLS), np.float32)
    c, s = rope_tables(pos, HD, RET_THETA)
    out[:, :, T_C:T_C + 64] = c.reshape(TILES, P, 64)
    out[:, :, T_S:T_S + 64] = s.reshape(TILES, P, 64)
    c, s = rope_tables(pos, ROPE_DIM, ROPE_THETA)
    out[:, :, T_CA:T_CA + 16] = c.reshape(TILES, P, 16)
    out[:, :, T_SA:T_SA + 16] = s.reshape(TILES, P, 16)
    q = np.arange(P)[:, None]
    k = np.arange(2 * P)[None, :]
    qc, kc = q // CHUNK + 2, k // CHUNK
    seen = (kc <= qc) & (kc >= qc - WINDOW // CHUNK)
    out[1:PROMPT_TILES, :, T_MASK:] = np.where(seen, 0, NEG)
    out[0, :, T_MASK:] = np.where(seen & (k >= P), 0, NEG)
    own = (k < P) | ((k - P) // DEC == q // DEC)
    out[SAMPLE, :, T_MASK:] = np.where(own, 0, NEG)
    return out


def mode_tables():
    log_g = np.log1p(-np.exp2(-5.0 - np.arange(HEADS)))
    i = np.arange(P)
    out = np.zeros((2, P, M_COLS), np.float32)
    for mode, span in enumerate((P, DEC)):
        chunk = CHUNK if mode == 0 else DEC
        j_, i_ = i[:, None], i[None, :]
        if mode == 0:
            seen = (j_ // chunk <= i_ // chunk)
        else:
            seen = (j_ // chunk == i_ // chunk)
        for h in range(HEADS):
            p, r = h // 2, h % 2
            m = np.where(seen, np.exp(log_g[h] * np.abs(i_ - j_)), 0) * HD ** -0.5
            out[mode, :, M_MASK + (r * 4 + p) * P:M_MASK + (r * 4 + p + 1) * P] = m
            dq = np.exp(log_g[h] * (i % span + 1.0))
            out[mode, 64 * r:64 * r + 64, M_DQ + p * P:M_DQ + (p + 1) * P] = dq[None, :]
            out[mode, :, M_DK + h] = np.exp(log_g[h] * (span - 1.0 - i % span)) * HD ** -0.5
            out[mode, 64 * r:64 * r + 64, M_G + p] = np.exp(log_g[h] * span)
    return out


def spread(ap, axis, n):
    a = ap.unsqueeze(axis)
    shape = list(a.shape)
    shape[axis] = n
    return a.to_broadcast(shape)


def wait_unless_0(eng, sem, value):
    if not isinstance(value, int) or value:
        eng.wait_ge(sem, value)


class Chain:

    def __init__(self, eng, sem, base=0):
        self.eng, self.sem, self.base, self.n = eng, sem, base, 0

    def after(self, ins):
        self.n += 1
        ins.then_inc(self.sem, 1)
        self.eng.wait_ge(self.sem, self.base + self.n)


def stage_mix(nc, psum, dr):
    X, TAB, MODE, WIN, WOUT = dr["x"], dr["tile_tab"], dr["mode_tab"], dr["w_in"], dr["w_out"]
    with ExitStack() as ctx:
        def sb(name, shape, dt=F32):
            return ctx.enter_context(nc.sbuf_tensor(name + "_sb", shape, dt))

        def sem(name):
            return ctx.enter_context(nc.semaphore(name))

        w_in = sb("w_in", [P, KC * IN_W])
        w_inv = w_in[:, :].rearrange("p (k n) -> p k n", k=KC)
        w_out = sb("w_out", [P, KC, D])
        ident = sb("ident", [P, P])
        gainT = sb("gainT", [P, KC])
        sinks = sb("sinks", [P, HEADS])
        mode = sb("mode", [P, M_COLS])
        tab = sb("tab", [P, T_COLS])
        XSLOTS = 3
        xt = sb("xt", [P, XSLOTS * D])
        xT = sb("xT", [P, KC, P])
        hT = sb("hT", [P, KC, P])
        zs = sb("zs", [P, IN_W])
        kd = sb("kd", [P, 512])
        kad = sb("kad", [P, KV, 2, HD])
        qT = sb("qT", [P, PAIRS, P])
        qTd = sb("qTd", [P, PAIRS, P])
        kT = sb("kT", [P, PAIRS, P])
        qaT = sb("qaT", [P, PAIRS, P])
        kaT = sb("kaT", [P, KV, 2, P])
        v_prev = sb("v_prev", [P, P])
        scT = sb("scT", [P, 2, PAIRS, P])
        S = sb("S", [P, PAIRS, P])
        sm = sb("sm", [P, HEADS, 2 * P])
        pT = sb("pT", [P, 2, HEADS, P])
        cat = sb("cat", [P, D])
        catT = sb("catT", [P, KC, P])
        ss = sb("ss", [P, 1])
        std = sb("std", [P, 1])
        rstd = sb("rstd", [P, 1])
        gsum = sb("gsum", [P, HEADS])
        gvar = sb("gvar", [P, HEADS])
        gstd = sb("gstd", [P, HEADS])
        grstd = sb("grstd", [P, HEADS])
        mx = sb("mx", [P, HEADS])
        nmx = sb("nmx", [P, HEADS])
        sk = sb("sk", [P, HEADS])
        ske = sb("ske", [P, HEADS])
        den = sb("den", [P, HEADS])
        rden = sb("rden", [P, HEADS])
        sm_flat = sm[:, :, :].rearrange("p h s -> p (h s)")
        rot = sm_flat[:, 0:1024]
        rota = sm_flat[:, 1024:1184].rearrange("p (h e) -> p h e", e=16)
        rotb = sm_flat[:, 1184:1344].rearrange("p (h e) -> p h e", e=16)
        qk = pT[:, 0, :, :].rearrange("p h t -> p (h t)")
        scT_flat = scT[:, :, :, :].rearrange("p r q t -> p (r q t)")
        dev = scT_flat[:, 0:512]
        dsq = scT_flat[:, 512:1024]

        def x_slot(t):
            return xt[:, bass.ds(t % XSLOTS * D, D)]

        def over(at, n):
            return w_in[:, at:at + n]

        kcT = over(0, 2048).rearrange("p (k b w) -> p k b w", k=KV, b=STREAMS)
        vc = over(2048, 1024).rearrange("p (b e) -> p b e", b=STREAMS)
        S0 = over(3072, 4096).rearrange("p (q b e) -> p q b e", q=PAIRS, b=STREAMS)
        qaTm = over(7168, 4096).rearrange("p (q b t) -> p q b t", q=PAIRS, b=STREAMS)
        qTdm = over(11264, 4096).rearrange("p (q b t) -> p q b t", q=PAIRS, b=STREAMS)
        vm = over(15360, 4096).rearrange("p (h b e) -> p h b e", h=HEADS, b=STREAMS)
        pTm = over(19456, 2048).rearrange("p (s b t) -> p s b t", s=2, b=STREAMS)
        bmask = over(21504, STREAMS)

        w_in_loaded = [sem(f"w_in_loaded{n}") for n in range(6)]
        w_out_loaded = sem("w_out_loaded")
        gain_loaded = sem("gain_loaded")
        sinks_loaded = sem("sinks_loaded")
        mode_loaded = sem("mode_loaded")
        sample_loaded = sem("sample_loaded")
        kcT_loaded = sem("kcT_loaded")
        x_loaded = sem("x_loaded")
        tab_loaded = sem("tab_loaded")
        ident_made = sem("ident_made")
        init_done = sem("init_done")
        act_step = sem("act_step")
        dve_step = sem("dve_step")
        std_ready = sem("std_ready")
        rstd_ready = sem("rstd_ready")
        xT_loaded = sem("xT_loaded")
        hT_ready = sem("hT_ready")
        z_psum = sem("z_psum")
        zs_ready = sem("zs_ready")
        rot_ready = sem("rot_ready")
        rota_ready = sem("rota_ready")
        qk_psum = sem("qk_psum")
        qkT_ready = sem("qkT_ready")
        qTd_ready = sem("qTd_ready")
        sc_psum = sem("sc_psum")
        scT_ready = sem("scT_ready")
        o_psum = sem("o_psum")
        st_psum = sem("st_psum")
        S_ready = sem("S_ready")
        gvar_ready = sem("gvar_ready")
        gstd_ready = sem("gstd_ready")
        sw_psum = sem("sw_psum")
        mx_ready = sem("mx_ready")
        p_ready = sem("p_ready")
        ske_ready = sem("ske_ready")
        pT_psum = sem("pT_psum")
        pT_ready = sem("pT_ready")
        pTm_ready = sem("pTm_ready")
        pTm_used = sem("pTm_used")
        oa_psum = sem("oa_psum")
        cat_ready = sem("cat_ready")
        catT_psum = sem("catT_psum")
        catT_ready = sem("catT_ready")
        y_psum = sem("y_psum")
        x1_ready = sem("x1_ready")
        x1_stored = sem("x1_stored")
        shifted = sem("shifted")
        masked_ready = sem("masked_ready")
        zeroed = sem("zeroed")
        out_stored = sem("out_stored")
        prompt_stored = sem("prompt_stored")

        Z_ORDER = ((0, 1), (1, 2), (4, 3), (5, 5), (2, 4), (3, 0))

        block = ctx.enter_context(nc.Block())

        @block.gpsimd
        def _(eng):
            eng.memset(ident[:, :], 0.0).then_inc(ident_made, 1)
            eng.wait_ge(ident_made, 1)
            eng.affine_select(out=ident[:, :], in_=ident[:, :], compare_op=ALU.not_equal, fill=1.0, base=0,
                              pattern=[[-1, P]], channel_multiplier=1).then_inc(ident_made, 1)
            eng.memset(S[:, :, :], 0.0).then_inc(init_done, 1)
            eng.memset(kaT[:, :, :, :], 0.0).then_inc(init_done, 1)
            eng.memset(v_prev[:, :], 0.0).then_inc(init_done, 1)

            def gain_applied(t):
                eng.wait_ge(xT_loaded, 16 * t + 16)
                wait_unless_0(eng, z_psum, 6 * t)
                eng.tensor_tensor(hT[:, :, :], xT[:, :, :], spread(gainT[:, :], 2, P), ALU.mult).then_inc(hT_ready, 1)

            eng.wait_ge(gain_loaded, 16)
            gain_applied(0)
            with eng.Fori(1, TILES) as t:
                gain_applied(t)
            eng.wait_ge(z_psum, 6 * TILES)
            eng.memset(qaTm, 0.0).then_inc(zeroed, 1)
            eng.memset(S0, 0.0).then_inc(zeroed, 1)
            eng.memset(qTdm, 0.0).then_inc(zeroed, 1)
            eng.memset(pTm, 0.0).then_inc(zeroed, 1)
            eng.memset(bmask, 1.0).then_inc(zeroed, 1)
            eng.wait_ge(zeroed, 5)
            eng.affine_select(out=bmask, in_=bmask, compare_op=ALU.is_ge, fill=0.0, base=0,
                              pattern=[[-DEC, STREAMS]], channel_multiplier=1).then_inc(zeroed, 1)
            eng.wait_ge(zeroed, 6)
            eng.affine_select(out=bmask, in_=bmask, compare_op=ALU.is_ge, fill=0.0, base=DEC - 1,
                              pattern=[[DEC, STREAMS]], channel_multiplier=-1).then_inc(zeroed, 1)

        @block.sync
        def _(eng):
            def x_in(t):
                eng.dma_start(x_slot(t), X[t]).then_inc(x_loaded, 16)

            def xT_in(t):
                src = dr["xT"][t]
                wait_unless_0(eng, hT_ready, t)
                eng.dma_start(xT[:, :, :], src).then_inc(xT_loaded, 16)

            def tab_in(t):
                eng.dma_start(tab[:, :], TAB[t]).then_inc(tab_loaded, 16)

            def x1_out(t):
                out = dr["x1"][t]
                x1 = x_slot(t)
                eng.wait_ge(x1_ready, t + 1)
                eng.dma_start(out, x1).then_inc(x1_stored, 16)

            def turn(t, more=True):
                xT_in(t + 1)
                table = TAB[t + 1]
                eng.wait_ge(mx_ready, t + 1)
                eng.dma_start(tab[:, :], table).then_inc(tab_loaded, 16)
                x1_out(t - 1)
                if more:
                    x_new = X[t + 2]
                    into = x_slot(t + 2)
                    eng.wait_ge(x1_stored, 16 * t)
                    eng.dma_start(into, x_new).then_inc(x_loaded, 16)

            xT_in(0)
            eng.dma_start(gainT[:, :], dr["norm_mixT"]).then_inc(gain_loaded, 16)
            x_in(0)
            tab_in(0)
            eng.dma_start(sinks[:, :], dr["sinks"].partition_broadcast(P)).then_inc(sinks_loaded, 16)
            eng.dma_start(mode[:, :], MODE[0]).then_inc(mode_loaded, 16)
            for t in (1, 2):
                eng.wait_ge(x_loaded, 16 * t)
                x_in(t)
            xT_in(1)
            eng.wait_ge(mx_ready, 1)
            tab_in(1)
            with eng.Fori(1, PROMPT_TILES - 1) as t:
                turn(t)
            turn(PROMPT_TILES - 1, False)
            eng.wait_ge(S_ready, 8 * PROMPT_TILES)
            eng.dma_start(dr["o_kp"], zs[:, Z_KA:Z_VA]).then_inc(prompt_stored, 16)
            eng.dma_start(dr["o_vp"], zs[:, Z_VA:IN_W]).then_inc(prompt_stored, 16)
            for r in range(2):
                eng.dma_start(dr["o_sp"].rearrange("(q r) d e -> r d q e", r=2)[r],
                              S[64 * r:64 * r + 64, :, 64 * r:64 * r + 64]).then_inc(prompt_stored, 16)
            eng.dma_start(mode[:, :], MODE[1]).then_inc(mode_loaded, 16)
            eng.wait_ge(z_psum, 6 * TILES)
            for r in range(2):
                eng.dma_start(kcT[64 * r:64 * r + 64], dr["kcT"]).then_inc(kcT_loaded, 16)
            eng.wait_ge(zeroed, 2)
            for r in range(2):
                for q in range(PAIRS):
                    eng.dma_start(S0[64 * r:64 * r + 64, q, :, 64 * r:64 * r + 64], dr["s0"][r, :, q])\
                       .then_inc(sample_loaded, 16)
            eng.dma_start(vc, dr["vc"].rearrange("b w e -> w b e")).then_inc(sample_loaded, 16)
            eng.dma_start(dr["o_ks"][:, 0:WINDOW - DEC, :], dr["kc"][:, DEC:WINDOW, :]).then_inc(out_stored, 16)
            eng.dma_start(dr["o_vs"][:, 0:WINDOW - DEC, :], dr["vc"][:, DEC:WINDOW, :]).then_inc(out_stored, 16)
            eng.wait_ge(rota_ready, 2 * TILES)
            for b in range(STREAMS):
                eng.dma_start(dr["o_ks"][b, WINDOW - DEC:, :], zs[DEC * b:DEC * (b + 1), Z_KA:Z_VA])\
                   .then_inc(out_stored, 16)
                eng.dma_start(dr["o_vs"][b, WINDOW - DEC:, :], zs[DEC * b:DEC * (b + 1), Z_VA:IN_W])\
                   .then_inc(out_stored, 16)
            eng.wait_ge(S_ready, 8 * TILES)
            for r in range(2):
                for q in range(PAIRS):
                    eng.dma_start(dr["o_ss"][r, :, q], S0[64 * r:64 * r + 64, q, :, 64 * r:64 * r + 64])\
                       .then_inc(out_stored, 16)
            x1_out(SAMPLE - 1)
            x1_out(SAMPLE)
            eng.wait_ge(x1_stored, 16 * TILES)
            eng.wait_ge(prompt_stored, 64)
            eng.wait_ge(out_stored, 16 * (2 + 2 * STREAMS + 2 * PAIRS))

        @block.tensor
        def _(eng):
            def bank(b, n=1):
                return psum[:, b * BANK:(b + n) * BANK]

            def cat_transposed(t):
                eng.wait_ge(cat_ready, t + 1)
                for k in range(KC):
                    mm = eng.transpose(bank(4, 2)[:, k * P:(k + 1) * P], cat[:, k * P:(k + 1) * P], ident[:, :])
                mm.then_inc(catT_psum, 1)

            def out_product(t):
                eng.wait_ge(catT_ready, t + 1)
                for n in range(2):
                    for k in range(KC):
                        mm = eng.matmul(bank(4 + n), catT[:, k, :], w_out[:, k, n * BANK:(n + 1) * BANK],
                                        start=(k == 0), stop=(k == KC - 1))
                mm.then_inc(y_psum, 1)

            def turn(t, first=False, second=False, sample=False):
                eng.wait_ge(hT_ready, t + 1)
                for i, (n, b) in enumerate(Z_ORDER):
                    if first:
                        eng.wait_ge(w_in_loaded[n], 16)
                    elif b == 5:
                        eng.wait_ge(S_ready, 8 * t)
                    elif b == 4:
                        eng.wait_ge(gvar_ready, t)
                    elif b == 0:
                        eng.wait_ge(cat_ready, t)
                    w = min(BANK, IN_W - n * BANK)
                    for k in range(KC):
                        mm = eng.matmul(bank(b)[:, 0:w], hT[:, k, :], w_inv[:, k, n * BANK:n * BANK + w],
                                        start=(k == 0), stop=(k == KC - 1))
                    mm.then_inc(z_psum, 1)
                eng.wait_ge(rot_ready, 2 * t + 2)
                for g in range(2):
                    for q in range(PAIRS):
                        mm = eng.transpose(bank(6 + g)[:, q * P:(q + 1) * P],
                                           qk[:, g * 512 + q * P:g * 512 + (q + 1) * P], ident[:, :])
                    mm.then_inc(qk_psum, 1)
                eng.wait_ge(rota_ready, 2 * t + 2)
                eng.wait_ge(zs_ready, 6 * t + 6)
                for q in range(PAIRS):
                    mm = eng.transpose(bank(0)[:, q * P:(q + 1) * P], zs[:, Z_QA + q * P:Z_QA + (q + 1) * P],
                                       ident[:, :])
                mm.then_inc(qk_psum, 1)
                for g in range(KV):
                    mm = eng.transpose(bank(1)[:, g * P:(g + 1) * P],
                                       kad[:, g, :, :].rearrange("p c e -> p (c e)"), ident[:, :])
                mm.then_inc(qk_psum, 1)
                if not first:
                    cat_transposed(t - 1)
                eng.wait_ge(qkT_ready, 4 * t + 4)
                for r in range(2):
                    for q in range(PAIRS):
                        s = slice(64 * r, 64 * r + 64)
                        mm = eng.matmul(bank(2 + r)[:, q * P:(q + 1) * P], kT[s, q, :], qT[s, q, :],
                                        start=True, stop=True)
                mm.then_inc(sc_psum, 1)
                if sample:
                    out_product(t - 1)
                    eng.wait_ge(masked_ready, 1)
                    eng.wait_ge(kcT_loaded, 32)
                for r in range(2):
                    for q in range(PAIRS):
                        s = slice(64 * r, 64 * r + 64)
                        out = bank((6, 0)[r], 2)[:, q * 256:(q + 1) * 256]
                        if not sample:
                            mm = eng.matmul(out, qaT[s, q, :], kaT[s, q // 2, :, :].rearrange("p c t -> p (c t)"),
                                            start=True, stop=True)
                        else:
                            for b in range(STREAMS):
                                eng.matmul(out[:, 0:P], qaTm[s, q, b, :], kcT[s, q // 2, b, :],
                                           start=(b == 0), stop=(b == STREAMS - 1))
                            mm = eng.matmul(out[:, P:2 * P], qaT[s, q, :], kaT[s, q // 2, 1, :],
                                            start=True, stop=True)
                mm.then_inc(sw_psum, 1)
                if not first:
                    if second:
                        eng.wait_ge(w_out_loaded, 16)
                    if not sample:
                        out_product(t - 1)
                eng.wait_ge(scT_ready, t + 1)
                for c in range(2):
                    for i in range(HEADS):
                        if c == 0:
                            eng.wait_ge(p_ready, 8 * t + i + 1)
                        mm = eng.transpose(bank((2, 6)[c], 2)[:, i * P:(i + 1) * P],
                                           sm[:, i, c * P:(c + 1) * P], ident[:, :])
                    mm.then_inc(pT_psum, 1)
                if not first:
                    eng.wait_ge(x1_ready, t)
                eng.wait_ge(rot_ready, 2 * t + 2)
                if not sample:
                    for q in range(PAIRS):
                        mm = eng.matmul(bank(5)[:, q * P:(q + 1) * P], kd[:, q * P:(q + 1) * P],
                                        zs[:, Z_V + q * P:Z_V + (q + 1) * P], start=True, stop=True)
                    mm.then_inc(st_psum, 1)
                eng.wait_ge(scT_ready, t + 1)
                eng.wait_ge(qTd_ready, t + 1)
                if sample:
                    eng.wait_ge(masked_ready, 2)
                    eng.wait_ge(sample_loaded, 16 * (1 + 2 * PAIRS))
                elif not first:
                    eng.wait_ge(S_ready, 8 * t)
                for q in range(PAIRS):
                    out = bank(4)[:, q * P:(q + 1) * P]
                    if not sample:
                        eng.matmul(out, qTd[:, q, :], S[:, q, :], start=True, stop=False)
                    else:
                        for b in range(STREAMS):
                            eng.matmul(out, qTdm[:, q, b, :], S0[:, q, b, :], start=(b == 0), stop=False)
                    for r in range(2):
                        hh = 2 * q + r
                        mm = eng.matmul(out[:, r * HD:(r + 1) * HD], scT[:, r, q, :],
                                        zs[:, Z_V + hh * HD:Z_V + (hh + 1) * HD], start=False, stop=(r == 1))
                mm.then_inc(o_psum, 1)
                if sample:
                    eng.wait_ge(masked_ready, 3)
                    for hh in range(HEADS):
                        q = hh // 2
                        if hh >= 1:
                            eng.wait_ge(S_ready, 8 * t + hh)
                        eng.matmul(bank(5), kd[:, q * P:(q + 1) * P],
                                   vm[:, hh].rearrange("p b e -> p (b e)"), start=True, stop=True)\
                           .then_inc(st_psum, 1)
                eng.wait_ge(pT_ready, 2 * t + 2)
                for hh in range(HEADS):
                    q, r = hh // 2, hh % 2
                    i, g = r * PAIRS + q, hh // 4
                    out = bank(0)[:, hh * HD:(hh + 1) * HD]
                    if not sample:
                        eng.matmul(out, pT[:, 0, i, :], v_prev[:, g * HD:(g + 1) * HD], start=True, stop=False)
                    else:
                        eng.wait_ge(pTm_ready, hh + 1)
                        for b in range(STREAMS):
                            mm = eng.matmul(out, pTm[:, hh % 2, b, :], vc[:, b, g * HD:(g + 1) * HD],
                                            start=(b == 0), stop=False)
                        mm.then_inc(pTm_used, 1)
                    mm = eng.matmul(out, pT[:, 1, i, :], zs[:, Z_VA + g * HD:Z_VA + (g + 1) * HD],
                                    start=False, stop=True)
                mm.then_inc(oa_psum, 1)

            eng.wait_ge(ident_made, 2)
            eng.wait_ge(init_done, 3)
            turn(0, first=True)
            turn(1, second=True)
            with eng.Fori(2, PROMPT_TILES) as t:
                turn(t)
            turn(SAMPLE, sample=True)
            cat_transposed(SAMPLE)
            out_product(SAMPLE)

        @block.scalar
        def _(eng):
            def mean_square(t):
                x = x_slot(t)
                eng.wait_ge(x_loaded, 16 * t + 16)
                Chain(eng, act_step, t).after(eng.activation(cat[:, :], x, ACT.Square, accum_out=ss[:, :]))
                eng.activation(std[:, :], ss[:, :], ACT.Sqrt, bias=EPS, scale=1.0 / D).then_inc(std_ready, 1)

            def catT_copy(t):
                eng.wait_ge(catT_psum, t + 1)
                eng.copy(catT[:, :, :].rearrange("p k t -> p (k t)"), psum[:, 4 * BANK:6 * BANK])\
                   .then_inc(catT_ready, 1)

            def turn(t, first=False, sample=False):
                eng.wait_ge(rstd_ready, t + 1)
                for i, (n, b) in enumerate(Z_ORDER):
                    w = min(BANK, IN_W - n * BANK)
                    eng.wait_ge(z_psum, 6 * t + i + 1)
                    if n == 5 and not first:
                        eng.wait_ge(shifted, t)
                    if sample and n == 4:
                        eng.wait_ge(prompt_stored, 64)
                    eng.activation(zs[:, n * BANK:n * BANK + w], psum[:, b * BANK:b * BANK + w],
                                   ACT.Silu if n == 3 else ACT.Copy, scale=rstd[:, 0:1]).then_inc(zs_ready, 1)
                for i, (src, dst) in enumerate(((6, qT), (7, kT), (0, qaT))):
                    eng.wait_ge(qk_psum, 4 * t + i + 1)
                    eng.copy(dst[:, :, :].rearrange("p q t -> p (q t)"), psum[:, src * BANK:(src + 1) * BANK])\
                       .then_inc(qkT_ready, 1)
                eng.wait_ge(qk_psum, 4 * t + 4)
                eng.copy(kaT[:, :, 1, :], psum[:, BANK:BANK + 256].rearrange("p (g t) -> p g t", g=KV))\
                   .then_inc(qkT_ready, 1)
                if not first:
                    catT_copy(t - 1)
                if not sample:
                    mean_square(t + 1)
                eng.wait_ge(mx_ready, t + 1)
                for i in range(HEADS):
                    eng.activation(sm[:, i, :], sm[:, i, :], ACT.Exp, bias=nmx[:, i:i + 1],
                                   accum_out=den[:, i:i + 1]).then_inc(p_ready, 1)
                eng.activation(ske[:, :], sk[:, :], ACT.Exp).then_inc(ske_ready, 1)
                for c in range(2):
                    eng.wait_ge(pT_psum, 2 * t + c + 1)
                    src = (2, 6)[c]
                    eng.copy(pT[:, c, :, :].rearrange("p h t -> p (h t)"), psum[:, src * BANK:(src + 2) * BANK])\
                       .then_inc(pT_ready, 1)
                eng.wait_ge(gvar_ready, t + 1)
                eng.activation(gstd[:, :], gvar[:, :], ACT.Sqrt, bias=EPS, scale=1.0 / HD).then_inc(gstd_ready, 1)

            for n, _ in Z_ORDER:
                cols = slice(n * BANK, min((n + 1) * BANK, IN_W))
                eng.dma_start(w_inv[:, :, cols], WIN.rearrange("(k p) n -> p k n", p=P)[:, :, cols])\
                   .then_inc(w_in_loaded[n], 16)
            eng.dma_start(w_out[:, :, :], WOUT.rearrange("(k p) n -> p k n", p=P)).then_inc(w_out_loaded, 16)
            mean_square(0)
            eng.wait_ge(init_done, 3)
            turn(0, first=True)
            with eng.Fori(1, PROMPT_TILES) as t:
                turn(t)
            turn(SAMPLE, sample=True)
            catT_copy(SAMPLE)

        @block.vector
        def _(eng):
            STEPS = 13

            def norm(t):
                eng.wait_ge(std_ready, t + 1)
                eng.reciprocal(rstd[:, :], std[:, :]).then_inc(rstd_ready, 1)

            def residual(t):
                eng.wait_ge(y_psum, t + 1)
                eng.tensor_tensor(x_slot(t), x_slot(t), psum[:, 4 * BANK:6 * BANK], ALU.add).then_inc(x1_ready, 1)

            def turn(t, first=False, sample=False):
                chain = Chain(eng, dve_step, STEPS * t)
                eng.wait_ge(tab_loaded, 16 * t + 16)
                eng.wait_ge(zs_ready, 6 * t + 2)
                if sample:
                    eng.wait_ge(mode_loaded, 32)
                z16 = zs[:, 0:1024].rearrange("p (h e) -> p h e", e=HD)
                qk16 = qk[:, :].rearrange("p (h e) -> p h e", e=HD)
                rot16 = rot[:, :].rearrange("p (h e) -> p h e", e=HD)
                eng.tensor_tensor(qk16, z16, spread(tab[:, T_C:T_C + HD], 1, 16), ALU.mult)
                eng.tensor_tensor(rot16[:, :, 0:32], z16[:, :, 32:64], spread(tab[:, T_S:T_S + 32], 1, 16), ALU.mult)
                chain.after(eng.tensor_tensor(rot16[:, :, 32:64], z16[:, :, 0:32],
                                              spread(tab[:, T_S + 32:T_S + 64], 1, 16), ALU.mult))
                eng.tensor_tensor(qk[:, :], qk[:, :], rot[:, :], ALU.add).then_inc(rot_ready, 1)
                eng.wait_ge(rot_ready, 2 * t + 1)
                eng.tensor_tensor(kd[:, :].rearrange("p (h e) -> p h e", e=HD), qk16[:, HEADS:, :],
                                  spread(mode[:, M_DK:M_DK + HEADS], 2, HD), ALU.mult).then_inc(rot_ready, 1)
                eng.wait_ge(zs_ready, 6 * t + 4)
                za = zs[:, Z_QA:Z_VA].rearrange("p (h e) -> p h e", e=HD)
                eng.tensor_tensor(rota[:, :, :], za[:, :, 0:16], spread(tab[:, T_CA:T_CA + 16], 1, 10), ALU.mult)
                eng.tensor_tensor(rotb[:, :, 0:8], za[:, :, 8:16], spread(tab[:, T_SA:T_SA + 8], 1, 10), ALU.mult)
                chain.after(eng.tensor_tensor(rotb[:, :, 8:16], za[:, :, 0:8],
                                              spread(tab[:, T_SA + 8:T_SA + 16], 1, 10), ALU.mult))
                eng.tensor_tensor(za[:, :, 0:16], rota[:, :, :], rotb[:, :, :], ALU.add).then_inc(rota_ready, 1)
                eng.wait_ge(rota_ready, 2 * t + 1)
                eng.tensor_copy(kad[:, :, :, :], spread(zs[:, Z_KA:Z_VA].rearrange("p (g e) -> p g e", g=KV), 2, 2))\
                   .then_inc(rota_ready, 1)
                eng.wait_ge(qkT_ready, 4 * t + 1)
                qd = eng.tensor_tensor(qTd[:, :, :].rearrange("p q t -> p (q t)"),
                                       qT[:, :, :].rearrange("p q t -> p (q t)"), mode[:, M_DQ:M_DK], ALU.mult)
                if not sample:
                    qd.then_inc(qTd_ready, 1)
                else:
                    qd.then_inc(qTd_ready, 1)
                    eng.wait_ge(qTd_ready, t + 1)
                    eng.wait_ge(qkT_ready, 4 * t + 3)
                    for dst, src, zeros in ((qaTm, qaT, 1), (qTdm, qTd, 3)):
                        eng.wait_ge(zeroed, zeros)
                        for q in range(PAIRS):
                            own = bass.AP(dst.tensor, dst.offset + q * STREAMS * P,
                                          [dst.ap[0], [P + DEC, STREAMS], [1, DEC]])
                            last = eng.tensor_copy(own, src[:, q, :].rearrange("p (b i) -> p b i", i=DEC))
                        last.then_inc(masked_ready, 1)
                    eng.wait_ge(zeroed, 7)
                    eng.wait_ge(zs_ready, 6 * t + 5)
                    for hh in range(HEADS):
                        last = eng.tensor_tensor(vm[:, hh], spread(zs[:, Z_V + hh * HD:Z_V + (hh + 1) * HD], 1, STREAMS),
                                                 spread(bmask, 2, HD), ALU.mult)
                    last.then_inc(masked_ready, 1)
                eng.wait_ge(sc_psum, t + 1)
                eng.tensor_tensor(scT[:, :, :, :].rearrange("p r q t -> p (r q t)"), psum[:, 2 * BANK:4 * BANK],
                                  mode[:, M_MASK:M_DQ], ALU.mult).then_inc(scT_ready, 1)
                eng.wait_ge(sw_psum, t + 1)
                for r, b in ((0, 6), (1, 0)):
                    last = eng.scalar_tensor_tensor(
                        out=sm[:, 4 * r:4 * r + 4, :],
                        in0=psum[:, b * BANK:(b + 2) * BANK].rearrange("p (q s) -> p q s", q=PAIRS),
                        scalar=HD ** -0.5, in1=spread(tab[:, T_MASK:T_COLS], 1, PAIRS), op0=ALU.mult, op1=ALU.add)
                chain.after(last)
                chain.after(eng.tensor_reduce(mx[:, :], sm[:, :, :], AX.X, ALU.max))
                chain.after(eng.tensor_tensor(mx[:, :], mx[:, :], sinks[:, :], ALU.max))
                eng.tensor_tensor(sk[:, :], sinks[:, :], mx[:, :], ALU.subtract)
                eng.tensor_scalar(nmx[:, :], mx[:, :], -1.0, None, ALU.mult).then_inc(mx_ready, 1)
                if not first:
                    residual(t - 1)
                if not sample:
                    norm(t + 1)
                if not sample:
                    eng.wait_ge(st_psum, t + 1)
                    eng.wait_ge(o_psum, t + 1)
                    for q in range(PAIRS):
                        for r in range(2):
                            s = slice(64 * r, 64 * r + 64)
                            at = 5 * BANK + q * P + r * HD
                            eng.scalar_tensor_tensor(out=S[s, q, s], in0=S[s, q, s], scalar=mode[s, M_G + q:M_G + q + 1],
                                                     in1=psum[s, at:at + HD], op0=ALU.mult, op1=ALU.add)\
                               .then_inc(S_ready, 1)
                else:
                    eng.wait_ge(o_psum, t + 1)
                    for hh in range(HEADS):
                        q, r = hh // 2, hh % 2
                        s = slice(64 * r, 64 * r + 64)
                        eng.wait_ge(st_psum, t + hh + 1)
                        dst = S0[s, q, :, s]
                        eng.scalar_tensor_tensor(out=dst, in0=dst, scalar=mode[s, M_G + q:M_G + q + 1],
                                                 in1=psum[s, 5 * BANK:6 * BANK].rearrange("p (b e) -> p b e", e=HD),
                                                 op0=ALU.mult, op1=ALU.add)\
                           .then_inc(S_ready, 1)
                o8 = psum[:, 4 * BANK:5 * BANK].rearrange("p (h e) -> p h e", e=HD)
                dev8 = dev.rearrange("p (h e) -> p h e", e=HD)
                dsq8 = dsq.rearrange("p (h e) -> p h e", e=HD)
                chain.after(eng.tensor_reduce(gsum[:, :], o8, AX.X, ALU.add))
                chain.after(eng.scalar_tensor_tensor(out=dev8, in0=spread(gsum[:, :], 2, HD), scalar=-1.0 / HD,
                                                     in1=o8, op0=ALU.mult, op1=ALU.add))
                chain.after(eng.tensor_tensor(dsq, dev, dev, ALU.mult))
                eng.tensor_reduce(gvar[:, :], dsq8, AX.X, ALU.add).then_inc(gvar_ready, 1)
                eng.wait_ge(gstd_ready, t + 1)
                chain.after(eng.reciprocal(grstd[:, :], gstd[:, :]))
                chain.after(eng.tensor_tensor(dev8, dev8, spread(grstd[:, :], 2, HD), ALU.mult))
                eng.wait_ge(zs_ready, 6 * t + 6)
                chain.after(eng.tensor_tensor(cat[:, 0:512], dev, zs[:, Z_G:Z_QA], ALU.mult))
                eng.wait_ge(ske_ready, t + 1)
                chain.after(eng.tensor_tensor(den[:, :], den[:, :], ske[:, :], ALU.add))
                chain.after(eng.reciprocal(rden[:, :], den[:, :]))
                if sample:
                    for hh in range(HEADS):
                        i = (hh % 2) * PAIRS + hh // 2
                        if hh == 0:
                            eng.wait_ge(pT_ready, 2 * t + 2)
                        if hh >= 2:
                            eng.wait_ge(pTm_used, hh - 1)
                        own = bass.AP(pTm.tensor, pTm.offset + (hh % 2) * STREAMS * P,
                                      [pTm.ap[0], [P + DEC, STREAMS], [1, DEC]])
                        eng.tensor_copy(own, pT[:, 0, i, :].rearrange("p (b i) -> p b i", i=DEC))\
                           .then_inc(pTm_ready, 1)
                eng.wait_ge(oa_psum, t + 1)
                for r in range(2):
                    last = eng.tensor_tensor(
                        cat[:, 512:1024].rearrange("p (q r e) -> p q r e", r=2, e=HD)[:, :, r, :],
                        psum[:, 0:BANK].rearrange("p (q r e) -> p q r e", r=2, e=HD)[:, :, r, :],
                        spread(rden[:, 4 * r:4 * r + 4], 2, HD), ALU.mult)
                last.then_inc(cat_ready, 1)
                if not sample:
                    eng.tensor_copy(kaT[:, :, 0, :], kaT[:, :, 1, :])
                    eng.tensor_copy(v_prev[:, :], zs[:, Z_VA:IN_W]).then_inc(shifted, 1)
                assert chain.n == STEPS

            norm(0)
            eng.wait_ge(sinks_loaded, 16)
            eng.wait_ge(mode_loaded, 16)
            eng.wait_ge(init_done, 3)
            turn(0, first=True)
            with eng.Fori(1, PROMPT_TILES) as t:
                turn(t)
            turn(SAMPLE, sample=True)
            residual(SAMPLE)


class SearchChain(Chain):

    def __init__(self, eng, sem, base, column):
        super().__init__(eng, sem, base)
        self.column = column

    def hold(self):
        self.eng.tensor_copy(self.column[:, 0:1], self.column[:, 1:2])

    def after(self, ins):
        super().after(ins)
        self.hold()


def top16(eng, chain, values, spare, best, where, groups):
    for g in range(groups):
        last = eng.max(best[:, g, 0:8], values[:, g, :])
    chain.after(last)
    for g in range(groups):
        eng.max_index(where[:, g, 0:8], best[:, g, 0:8], values[:, g, :])
        last = eng.match_replace(spare[:, g, :], best[:, g, 0:8], values[:, g, :], LOWEST)
    chain.after(last)
    for g in range(groups):
        last = eng.max(best[:, g, 8:16], spare[:, g, :])
    chain.after(last)
    for g in range(groups):
        last = eng.max_index(where[:, g, 8:16], best[:, g, 8:16], spare[:, g, :])
    chain.after(last)


def stage_route(nc, psum, dr, chosenT):
    with ExitStack() as ctx:
        def sb(name, shape, dt=F32):
            return ctx.enter_context(nc.sbuf_tensor("r_" + name, shape, dt))

        def sem(name):
            return ctx.enter_context(nc.semaphore("r_" + name))

        w_q = sb("w_q", [P, KC, SIDES * P])
        keys = sb("keys", [P, SIDES, NKEYS])
        gain = sb("gain", [P, D])
        ident = sb("ident", [P, P])
        xt = sb("xt", [P, D])
        h = sb("h", [P, D])
        hT = sb("hT", [P, KC, P])
        qT = sb("qT", [P, SIDES, P])
        s = sb("s", [P, SIDES, NKEYS])
        spare = sb("spare", [P, SIDES * NKEYS])
        cand = sb("cand", [P, PEER_HEADS, CANDS])
        best = sb("best", [P, SIDES, TOPK])
        where = sb("where", [P, SIDES, TOPK], U32)
        wheref = sb("wheref", [P, SIDES, TOPK], BF16)
        rowstep = sb("rowstep", [P, PEER_HEADS, TOPK], BF16)
        starts = sb("starts", [P, TOPK], BF16)
        sc = sb("sc", [P, PEER_HEADS, TOPK])
        sel = sb("sel", [P, PEER_HEADS, TOPK], U32)
        width = sb("width", [P, 3, CHOSEN])
        mask = sb("mask", [P, CHOSEN], U32)
        rank = sb("rank", [P, CHOSEN], U32)
        repeated = sb("repeated", [P, 2, CHOSEN, TOPK], BF16)
        iota = sb("iota", [P, TOPK], BF16)
        eq = sb("eq", [P, CHOSEN, TOPK], BF16)
        squares = sb("squares", [P, D])
        chosen = sb("chosen", [P, 3, CHOSEN])
        e = sb("e", [P, PEER_HEADS, TOPK])
        esum = sb("esum", [P, PEER_HEADS])
        ss = sb("ss", [P, 1])
        std = sb("std", [P, 1])
        rstd = sb("rstd", [P, 1])
        held = sb("held", [P, 2])

        w_q_loaded = [sem(f"w_q_loaded{g}") for g in range(4)]
        keys_loaded = sem("keys_loaded")
        gain_loaded = sem("gain_loaded")
        made = sem("made")
        starts_made = sem("starts_made")
        held_made = sem("held_made")
        x_loaded = sem("x_loaded")
        act_step = sem("act_step")
        dve_step = sem("dve_step")
        std_ready = sem("std_ready")
        h_ready = sem("h_ready")
        hT_psum = sem("hT_psum")
        hT_ready = sem("hT_ready")
        hT_stored = sem("hT_stored")
        q_psum = sem("q_psum")
        qT_ready = sem("qT_ready")
        s_psum = sem("s_psum")
        s_ready = sem("s_ready")
        s_used = sem("s_used")
        sc_ready = sem("sc_ready")
        e_ready = sem("e_ready")
        rank_ready = sem("rank_ready")
        repeated_ready = sem("repeated_ready")
        chosen_ready = sem("chosen_ready")
        chosen_psum = sem("chosen_psum")
        chosenT_ready = sem("chosenT_ready")

        block = ctx.enter_context(nc.Block())

        @block.gpsimd
        def _(eng):
            eng.memset(ident[:, :], 0.0).then_inc(made, 1)
            eng.wait_ge(made, 1)
            eng.affine_select(out=ident[:, :], in_=ident[:, :], compare_op=ALU.not_equal, fill=1.0, base=0,
                              pattern=[[-1, P]], channel_multiplier=1).then_inc(made, 1)
            eng.iota(iota[:, :], pattern=[[1, TOPK]], base=0, channel_multiplier=0,
                     allow_small_or_imprecise_dtypes=True).then_inc(made, 1)
            for a, n, step in ((0, 1, 1), (1, 4, 8), (5, 3, 4), (8, 8, 1)):
                eng.iota(starts[:, a:a + n], pattern=[[step, n]], base=START[a], channel_multiplier=0,
                         allow_small_or_imprecise_dtypes=True).then_inc(starts_made, 1)

        @block.sync
        def _(eng):
            def load(t):
                eng.dma_start(xt[:, :], dr["x1"][t]).then_inc(x_loaded, 16)

            load(0)
            eng.dma_start(gain[:, :], dr["norm_ffn"].partition_broadcast(P)).then_inc(gain_loaded, 16)
            with eng.Fori(0, TILES - 1) as t:
                eng.wait_ge(h_ready, t + 1)
                load(t + 1)
                eng.wait_ge(hT_ready, t + 1)
                eng.dma_start(dr["h2T"][t], hT[:, :, :]).then_inc(hT_stored, 16)
            eng.wait_ge(hT_ready, TILES)
            eng.dma_start(dr["h2T"][TILES - 1], hT[:, :, :]).then_inc(hT_stored, 16)
            eng.wait_ge(hT_stored, 16 * TILES)

        @block.tensor
        def _(eng):
            def front(t, first=False, second=False):
                eng.wait_ge(h_ready, t + 1)
                if not first:
                    eng.wait_ge(s_ready, t * 4)
                for k in range(KC):
                    mm = eng.transpose(psum[:, k * P:(k + 1) * P], h[:, k * P:(k + 1) * P], ident[:, :])
                mm.then_inc(hT_psum, 1)
                eng.wait_ge(hT_ready, t + 1)
                if not (first or second):
                    eng.wait_ge(chosenT_ready, t - 1)
                for g in range(4):
                    if first:
                        eng.wait_ge(w_q_loaded[g], 16)
                    for i in range(4):
                        at = 4 * g + i
                        out = psum[:, (2 + g) * BANK + i * P:(2 + g) * BANK + (i + 1) * P]
                        for k in range(KC):
                            mm = eng.matmul(out, w_q[:, k, at * P:(at + 1) * P], hT[:, k, :],
                                            start=(k == 0), stop=(k == KC - 1))
                    mm.then_inc(q_psum, 1)
                if first:
                    eng.wait_ge(keys_loaded, 16)
                for g in range(4):
                    eng.wait_ge(qT_ready, 4 * t + g + 1)
                    for i in range(4):
                        at = 4 * g + i
                        b = (6, 7, 0, 1)[g]
                        mm = eng.matmul(psum[:, b * BANK + i * P:b * BANK + (i + 1) * P], qT[:, at, :],
                                        keys[:, at, :], start=True, stop=True)
                    mm.then_inc(s_psum, 1)

            def back(t):
                eng.wait_ge(chosen_ready, t + 1)
                for c in range(3):
                    mm = eng.transpose(psum[:, 2 * BANK + c * P:2 * BANK + (c + 1) * P], chosen[:, c, :], ident[:, :])
                mm.then_inc(chosen_psum, 1)

            eng.wait_ge(made, 3)
            front(0, first=True)
            front(1, second=True)
            back(0)
            with eng.Fori(2, TILES) as t:
                front(t)
                back(t - 1)
            back(TILES - 1)

        @block.scalar
        def _(eng):
            def softmax_and_places(t):
                eng.wait_ge(sc_ready, t + 1)
                eng.copy(repeated[:, 0, :, :], spread(sel[:, :, :].rearrange("p h k -> p (h k)"), 2, TOPK))\
                   .then_inc(repeated_ready, 1)
                eng.activation(e[:, :, :], e[:, :, :], ACT.Exp).then_inc(e_ready, 1)
                eng.wait_ge(rank_ready, t + 1)
                eng.copy(repeated[:, 1, :, :], spread(rank[:, :], 2, TOPK)).then_inc(repeated_ready, 1)

            def mean_square(t):
                eng.wait_ge(x_loaded, 16 * t + 16)
                Chain(eng, act_step, t).after(eng.activation(squares[:, :], xt[:, :], ACT.Square, accum_out=ss[:, :]))
                eng.activation(std[:, :], ss[:, :], ACT.Sqrt, bias=EPS, scale=1.0 / D).then_inc(std_ready, 1)

            def front(t, first=False, last=False):
                eng.wait_ge(hT_psum, t + 1)
                if not first:
                    eng.wait_ge(hT_stored, 16 * t)
                eng.copy(hT[:, :, :].rearrange("p k t -> p (k t)"), psum[:, 0:2 * BANK]).then_inc(hT_ready, 1)
                for g in range(4):
                    eng.wait_ge(q_psum, 4 * t + g + 1)
                    eng.copy(qT[:, 4 * g:4 * g + 4, :].rearrange("p s t -> p (s t)"),
                             psum[:, (2 + g) * BANK:(3 + g) * BANK]).then_inc(qT_ready, 1)
                    if g == 0 and not last:
                        mean_square(t + 1)
                    if g == 1 and not first:
                        softmax_and_places(t - 1)
                if not first:
                    eng.wait_ge(s_used, t)
                for g in range(4):
                    b = (6, 7, 0, 1)[g]
                    eng.wait_ge(s_psum, 4 * t + g + 1)
                    eng.copy(s[:, 4 * g:4 * g + 4, :].rearrange("p s t -> p (s t)"),
                             psum[:, b * BANK:(b + 1) * BANK]).then_inc(s_ready, 1)

            def back(t):
                eng.wait_ge(chosen_psum, t + 1)
                eng.copy(chosenT[:, :, bass.ds(t * P, P)],
                         psum[:, 2 * BANK:2 * BANK + 3 * P].rearrange("p (c t) -> p c t", c=3))\
                   .then_inc(chosenT_ready, 1)

            for g in range(4):
                cols = slice(4 * g * P, 4 * (g + 1) * P)
                eng.dma_start(w_q[:, :, cols], dr["w_q"].rearrange("(k p) n -> p k n", p=P)[:, :, cols])\
                   .then_inc(w_q_loaded[g], 16)
            eng.dma_start(keys[:, :, :], dr["keysT"]).then_inc(keys_loaded, 16)
            mean_square(0)
            front(0, first=True)
            with eng.Fori(1, TILES - 1) as t:
                front(t)
                back(t - 1)
            front(TILES - 1, last=True)
            back(TILES - 2)
            softmax_and_places(TILES - 1)
            back(TILES - 1)

        @block.vector
        def _(eng):
            STEPS = 21

            def front(t, chain):
                eng.wait_ge(std_ready, t + 1)
                chain.after(eng.reciprocal(rstd[:, :], std[:, :]))
                eng.scalar_tensor_tensor(out=h[:, :], in0=xt[:, :], scalar=rstd[:, 0:1], in1=gain[:, :],
                                         op0=ALU.mult, op1=ALU.mult).then_inc(h_ready, 1)

            def back(t, base, first=False, more=True):
                search = SearchChain(eng, dve_step, base, held)
                eng.wait_ge(s_ready, 4 * t + 4)
                search.hold()
                top16(eng, search, s[:, :, :], spare[:, :].rearrange("p (g n) -> p g n", g=SIDES),
                      best[:, :, :], where[:, :, :], SIDES)
                pair = best[:, :, :].rearrange("p (h c) r -> p h c r", c=2)
                eng.tensor_copy(wheref[:, :, :], where[:, :, :]).then_inc(s_used, 1)
                for a, na, nb in CAND_RECTS:
                    last = eng.tensor_tensor(
                        cand[:, :, START[a]:START[a] + na * nb].rearrange("p h (a b) -> p h a b", a=na),
                        spread(pair[:, :, 0, a:a + na], 3, nb), spread(pair[:, :, 1, 0:nb], 2, na), ALU.add)
                search.after(last)
                top16(eng, search, cand[:, :, :],
                      spare[:, 0:PEER_HEADS * CANDS].rearrange("p (g n) -> p g n", g=PEER_HEADS),
                      sc[:, :, :], sel[:, :, :], PEER_HEADS)
                chain = Chain(eng, dve_step, base + search.n)
                eng.tensor_tensor(e[:, :, :], sc[:, :, :], sc[:, :, 0:1].to_broadcast([P, PEER_HEADS, TOPK]),
                                  ALU.subtract).then_inc(sc_ready, 1)
                place = sel[:, :, :].rearrange("p h k -> p (h k)")
                for i, (below, bits) in enumerate(((START[1], 8.0), (START[4], 4.0), (START[8], 3.0))):
                    eng.tensor_scalar(width[:, i, :], place, below, bits, ALU.is_lt, ALU.mult)
                sides = wheref[:, :, :].rearrange("p (h c) r -> p h c r", c=2)
                eng.tensor_copy(rowstep[:, :, 0:1], sides[:, :, 0, 0:1])
                chain.after(eng.tensor_tensor(rowstep[:, :, 1:TOPK], sides[:, :, 0, 1:TOPK], sides[:, :, 0, 0:TOPK - 1],
                                              ALU.subtract))
                chain.after(eng.tensor_tensor(width[:, 0, :], width[:, 0, :], width[:, 1, :], ALU.add))
                chain.after(eng.tensor_tensor(mask[:, :], width[:, 0, :], width[:, 2, :], ALU.add))
                eng.tensor_tensor(rank[:, :], place, mask[:, :], ALU.bitwise_and).then_inc(rank_ready, 1)
                if more:
                    front(t + 2, chain)
                eq4 = eq[:, :, :].rearrange("p (h k) r -> p h k r", h=PEER_HEADS)
                if not first:
                    eng.wait_ge(chosen_psum, t)
                for c, (table, test, value) in enumerate(((starts, ALU.is_ge, rowstep[:, :, :]),
                                                          (iota, ALU.is_equal, sides[:, :, 1, :]))):
                    eng.wait_ge(repeated_ready, 2 * t + c + 1)
                    chain.after(eng.tensor_tensor(eq[:, :, :], repeated[:, c, :, :], spread(table[:, :], 1, CHOSEN),
                                                  test))
                    chain.after(eng.tensor_tensor(eq4, eq4, spread(value, 2, TOPK), ALU.mult))
                    chain.after(eng.tensor_reduce(chosen[:, c, :], eq[:, :, :], AX.X, ALU.add))
                eng.wait_ge(e_ready, t + 1)
                chain.after(eng.tensor_reduce(esum[:, :], e[:, :, :], AX.X, ALU.add))
                chain.after(eng.reciprocal(esum[:, :], esum[:, :]))
                eng.tensor_tensor(chosen[:, 2, :].rearrange("p (h k) -> p h k", h=PEER_HEADS), e[:, :, :],
                                  spread(esum[:, :], 2, TOPK), ALU.mult).then_inc(chosen_ready, 1)
                assert search.n + chain.n == STEPS - (not more)

            eng.wait_ge(gain_loaded, 16)
            eng.wait_ge(made, 3)
            eng.wait_ge(starts_made, 4)
            eng.memset(held[:, :], 0.0).then_inc(held_made, 1)
            eng.wait_ge(held_made, 1)
            start = Chain(eng, dve_step)
            front(0, start)
            front(1, start)
            back(0, start.n, first=True)
            with eng.Fori(1, TILES - 2) as t:
                back(t, STEPS * t + start.n)
            back(TILES - 2, STEPS * (TILES - 2) + start.n, more=False)
            back(TILES - 1, STEPS * (TILES - 1) + start.n - 1, more=False)


def stage_gates(nc, psum, dr, chosenT, shared):
    GROUP = 8
    ON_POOL, ON_ACT = 4, 3
    with ExitStack() as ctx:
        def sb(name, shape, dt=F32):
            return ctx.enter_context(nc.sbuf_tensor("g_" + name, shape, dt))

        def sem(name):
            return ctx.enter_context(nc.semaphore("g_" + name))

        iota = sb("iota", [P, P])
        rows = [sb(f"rows{i}", [P, GROUP, P]) for i in range(2)]
        cols = [sb(f"cols{i}", [P, GROUP, P]) for i in range(2)]
        held = sb("held", [P, 4])
        pool_cols = sb("pool_cols", [P, 2, ON_POOL])
        dist = sb("dist", [P, 2, ON_ACT, P])
        grid = [sb("grid", [P, NKEYS, GATE_CHUNK]), shared.grid]

        made = sem("made")
        onehot_ready = sem("onehot_ready")
        held_made = sem("held_made")
        pool_cols_chosen = sem("pool_cols_chosen")
        pool_cols_ready = sem("pool_cols_ready")
        dist_ready = sem("dist_ready")
        act_cols_ready = sem("act_cols_ready")
        grid_psum = sem("grid_psum")
        grid_ready = sem("grid_ready")
        grid_stored = [sem("grid_stored"), shared.grid_stored]
        GROUPS = GATE_CHUNK // GROUP
        CHUNKS = BTOK // GATE_CHUNK

        block = ctx.enter_context(nc.Block())

        @block.gpsimd
        def _(eng):
            eng.iota(iota[:, :], pattern=[[1, P]], base=0, channel_multiplier=0,
                     allow_small_or_imprecise_dtypes=True).then_inc(made, 1)
            eng.wait_ge(made, 1)
            eng.memset(held[:, :], 0.0).then_inc(held_made, 1)
            eng.wait_ge(held_made, 1)

            def group(g, i, first):
                eng.wait_ge(pool_cols_chosen, g + 1)
                eng.tensor_tensor(held[:, i:i + 1], held[:, 2:3], held[:, 3:4], ALU.add)
                for n in range(ON_POOL):
                    last = eng.tensor_scalar(cols[i][:, n, :], iota[:, :], pool_cols[:, i, n:n + 1], None, ALU.is_equal)
                last.then_inc(pool_cols_ready, 1)

            group(0, 0, True)
            group(1, 1, True)
            with eng.Fori(1, CHUNKS * GROUPS // 2) as m:
                group(m * 2, 0, False)
                group(m * 2 + 1, 1, False)

        @block.vector
        def _(eng):
            def group(g, i, first):
                if not first:
                    eng.wait_ge(grid_psum, g - 1)
                eng.tensor_copy(pool_cols[:, i, :], chosenT[:, 1, bass.ds(g * GROUP, ON_POOL)])\
                   .then_inc(pool_cols_chosen, 1)
                for n in range(ON_POOL + ON_ACT, GROUP):
                    eng.tensor_scalar(cols[i][:, n, :], iota[:, :], chosenT[:, 1, bass.ds(g * GROUP + n, 1)], None,
                                      ALU.is_equal)
                for n in range(GROUP):
                    at = g * GROUP + n
                    last = eng.tensor_scalar(rows[i][:, n, :], iota[:, :], chosenT[:, 0, bass.ds(at, 1)],
                                             chosenT[:, 2, bass.ds(at, 1)], ALU.is_equal, ALU.mult)
                last.then_inc(onehot_ready, 1)

            eng.wait_ge(made, 1)
            group(0, 0, True)
            group(1, 1, True)
            with eng.Fori(1, CHUNKS * GROUPS // 2) as m:
                group(m * 2, 0, False)
                group(m * 2 + 1, 1, False)

        @block.tensor
        def _(eng):
            def group(g, i, first):
                eng.wait_ge(onehot_ready, g + 1)
                eng.wait_ge(pool_cols_ready, g + 1)
                eng.wait_ge(act_cols_ready, g + 1)
                if not first:
                    eng.wait_ge(grid_ready, g - 1)
                for n in range(GROUP):
                    mm = eng.matmul(psum[:, 2 * i * BANK + n * P:2 * i * BANK + (n + 1) * P], rows[i][:, n, :],
                                    cols[i][:, n, :], start=True, stop=True)
                mm.then_inc(grid_psum, 1)

            group(0, 0, True)
            group(1, 1, True)
            with eng.Fori(1, CHUNKS * GROUPS // 2) as m:
                group(m * 2, 0, False)
                group(m * 2 + 1, 1, False)

        @block.scalar
        def _(eng):
            def onehots(g, i):
                for n in range(ON_ACT):
                    at = g * GROUP + ON_POOL + n
                    last = eng.activation(dist[:, i, n, :], iota[:, :], ACT.Abs, bias=chosenT[:, 1, bass.ds(at, 1)],
                                          scale=-1.0)
                last.then_inc(dist_ready, 1)
                eng.wait_ge(dist_ready, g + 1)
                eng.activation(cols[i][:, ON_POOL:ON_POOL + ON_ACT, :], dist[:, i, :, :], ACT.Relu, bias=1.0, scale=-1.0)\
                   .then_inc(act_cols_ready, 1)

            def group(c, g, i, slot, onward=True):
                eng.wait_ge(grid_psum, c * GROUPS + g + 1)
                eng.copy(grid[slot][:, :, bass.ds(g * GROUP, GROUP)],
                         psum[:, 2 * i * BANK:(2 * i + 2) * BANK].rearrange("p (t j) -> p j t", t=GROUP))\
                   .then_inc(grid_ready, 1)
                if onward:
                    onehots(c * GROUPS + g + 2, i)

            eng.wait_ge(made, 1)
            onehots(0, 0)
            onehots(1, 1)
            for c in range(CHUNKS):
                last = c == CHUNKS - 1
                if c >= 2:
                    eng.wait_ge(grid_stored[c % 2], 16 * (c // 2))
                with eng.Fori(0, GROUPS // 2 - last) as m:
                    group(c, m * 2, 0, c % 2)
                    group(c, m * 2 + 1, 1, c % 2)
                if last:
                    group(c, GROUPS - 2, 0, c % 2, False)
                    group(c, GROUPS - 1, 1, c % 2, False)

        @block.sync
        def _(eng):
            shared.load(eng, dr)
            for c in range(CHUNKS):
                eng.wait_ge(grid_ready, GROUPS * (c + 1))
                eng.dma_start(dr["gates"][c], grid[c % 2][:, :, :]).then_inc(grid_stored[c % 2], 16)
            eng.wait_ge(grid_stored[0], 16 * (CHUNKS // 2))


class Shared:

    def __init__(self, nc, ctx):
        def sb(name, shape):
            return ctx.enter_context(nc.sbuf_tensor("e_" + name, shape, F32))

        def sem(name):
            return ctx.enter_context(nc.semaphore("e_" + name))

        self.h_raw = sb("h_raw", [P, BT, KC, P])
        self.u_raw = [sb(f"u_raw{i}", [P, D]) for i in range(2)]
        self.v_raw = [sb(f"v_raw{i}", [P, D]) for i in range(2)]
        self.grid = sb("grid", [P, NKEYS, GATE_CHUNK])
        self.grid_stored = sem("first_grids_stored")
        self.h_loaded = sem("h_loaded")
        self.u_loaded = [sem(f"u_loaded{i}") for i in range(2)]
        self.v_loaded = [sem(f"v_loaded{i}") for i in range(2)]

    def load(self, eng, dr):
        for i in range(2):
            eng.dma_start(self.u_raw[i][:, :], dr["uT"][i]).then_inc(self.u_loaded[i], 16)
        eng.dma_start(self.h_raw[:, :, :, :].rearrange("p t k q -> p t (k q)"),
                      dr["h2T"][0:BT].rearrange("t p n -> p t n")).then_inc(self.h_loaded, 16)
        eng.dma_start(self.v_raw[0][:, :], dr["v"][:, 0, :]).then_inc(self.v_loaded[0], 16)


def stage_experts(nc, psum, dr, chosenT, shared):
    COLS = NKEYS
    UNROLL = 4
    TURNS = COLS // UNROLL
    GROUP = 4
    CHUNK_TURNS = GATE_CHUNK // GROUP // UNROLL
    PERIOD = CHUNK_TURNS + 1
    CHUNKS = BTOK // GATE_CHUNK
    GROUPS = BTOK // GROUP
    assert CHUNKS * PERIOD <= TURNS - 1
    with ExitStack() as ctx:
        def sb(name, shape, dt=F32):
            return ctx.enter_context(nc.sbuf_tensor("e_" + name, shape, dt))

        def sem(name):
            return ctx.enter_context(nc.semaphore("e_" + name))

        gain = sb("gain", [P, D])
        h_hi = [sb(f"h_hi{i}", [P, KC, BT, P], F32R) for i in range(2)]
        h_lo = [sb(f"h_lo{i}", [P, KC, BT, P], F32R) for i in range(2)]
        h_raw, u_raw, v_raw = shared.h_raw, shared.u_raw, shared.v_raw
        h_loaded, u_loaded, v_loaded = shared.h_loaded, shared.u_loaded, shared.v_loaded
        g_raw = [sb(f"g_raw{i}", [P, CHUNKS, GATE_CHUNK]) for i in range(2)]
        u_hi = [sb(f"u_hi{i}", [P, D], F32R) for i in range(2)]
        u_lo = [sb(f"u_lo{i}", [P, D], F32R) for i in range(2)]
        v_hi = [sb(f"v_hi{i}", [P, D], F32R) for i in range(2)]
        v_lo = [sb(f"v_lo{i}", [P, D], F32R) for i in range(2)]
        gl = [sb(f"gl{i}", [P, BTOK]) for i in range(2)]
        a = [sb(f"a{i}", [P, BTOK]) for i in range(2)]
        a_hi = [sb(f"a_hi{i}", [P, BTOK], F32R) for i in range(2)]
        a_lo = [sb(f"a_lo{i}", [P, BTOK], F32R) for i in range(2)]
        y = sb("y", [P, BT, D])
        sq = h_raw[:, :, :, :].rearrange("p t k q -> p t (k q)")
        ss = sb("ss", [P, BT])
        std = sb("std", [P, BT])
        rstd = sb("rstd", [P, BT])
        PARTS = 3
        iota = sb("iota", [P, P], BF16)
        rounded = sb("rounded", [P, (BLOCKS - 1) * BTOK], BF16)
        gate_part = sb("gate_part", [P, PARTS, (BLOCKS - 1) * BTOK])
        rows = sb("rows", [P, GROUP, PARTS, P], BF16)
        cols = sb("cols", [P, GROUP, P], BF16)
        grid = shared.grid

        gain_loaded = sem("gain_loaded")
        iota_made = sem("iota_made")
        part_step = sem("part_step")
        h_hi_ready = sem("h_hi_ready")
        h_ready = sem("h_ready")
        g_loaded = [sem(f"g_loaded{i}") for i in range(2)]
        u_hi_ready = sem("u_hi_ready")
        u_ready = sem("u_ready")
        v_hi_ready = sem("v_hi_ready")
        v_ready = sem("v_ready")
        s_done = sem("s_done")
        gl_ready = sem("gl_ready")
        dve_step = sem("dve_step")
        a_ready = sem("a_ready")
        o_done = sem("o_done")
        onehot_ready = sem("onehot_ready")
        grid_psum = sem("grid_psum")
        grid_ready = sem("grid_ready")
        grid_stored = sem("grid_stored")
        x1_loaded = sem("x1_loaded")
        sum_ready = sem("sum_ready")
        ss_ready = sem("ss_ready")
        std_ready = sem("std_ready")
        y_ready = sem("y_ready")
        y_stored = sem("y_stored")

        def each_column(eng, b, step, chunk_begin=None, chunk_end=None):
            def turn(n, group=None, place=None):
                for i in range(UNROLL):
                    step(n, i, *((None, None) if group is None else (group + i, place + i)))

            def call(part, k):
                if part:
                    part(k)

            if b == BLOCKS - 1:
                turn(0)
                with eng.Fori(1, TURNS - 1) as n:
                    turn(n)
                turn(TURNS - 1)
                return
            call(chunk_begin, 0)
            turn(0, 0, 0)
            with eng.Fori(1, CHUNK_TURNS) as n:
                turn(n, n * UNROLL, n * UNROLL)
            call(chunk_end, 0)
            turn(CHUNK_TURNS)
            with eng.Fori(1, CHUNKS) as k:
                call(chunk_begin, k)
                with eng.Fori(0, CHUNK_TURNS) as m:
                    turn(k * PERIOD + m, (k * CHUNK_TURNS + m) * UNROLL, m * UNROLL)
                call(chunk_end, k)
                turn(k * PERIOD + CHUNK_TURNS)
            for n in range(CHUNKS * PERIOD, TURNS):
                turn(n)

        LAST = TURNS - 1

        def in_last(n):
            return isinstance(n, int) and n == LAST

        def in_first(n):
            return isinstance(n, int) and n == 0

        def halves():
            return [(half, slice(half * KC // 2, (half + 1) * KC // 2)) for half in range(2)]

        block = ctx.enter_context(nc.Block())

        @block.gpsimd
        def _(eng):
            eng.iota(iota[:, :], pattern=[[1, P]], base=0, channel_multiplier=0,
                     allow_small_or_imprecise_dtypes=True).then_inc(iota_made, 1)

        @block.sync
        def _(eng):
            def u_in(j, i, used):
                src = dr["uT"][bass.ds(j, 1)].rearrange("j p n -> p j n")
                eng.wait_ge(u_ready, used)
                eng.dma_start(u_raw[i % 2][:, :].unsqueeze(1), src).then_inc(u_loaded[i % 2], 16)

            def v_in(j, i, used):
                src = dr["v"][:, bass.ds(j, 1), :]
                if used is not None:
                    eng.wait_ge(v_ready, used)
                eng.dma_start(v_raw[i % 2][:, :].unsqueeze(1), src).then_inc(v_loaded[i % 2], 16)

            def block_of_tokens(b):
                def step(n, i, group, place):
                    j = n * UNROLL + i
                    at = b * COLS + j
                    very_first = in_first(n) and b == 0
                    wrap = COLS if in_last(n) else 0
                    if not (in_last(n) and i >= 2 and b == BLOCKS - 1):
                        u_in(j + 2 - (wrap if i >= 2 else 0), i, at + 1)
                    if not (in_last(n) and i >= 3 and b == BLOCKS - 1):
                        v_in(j + 1 - (wrap if i >= 3 else 0), i + 1, None if very_first and i == 0 else at)
                    src = dr["gates"][b * CHUNKS:(b + 1) * CHUNKS, :, bass.ds(j, 1), :].rearrange("c p j q -> p c j q")
                    if in_first(n) and i == 0:
                        if b:
                            eng.wait_ge(grid_stored, 16 * CHUNKS * b)
                        else:
                            eng.wait_ge(shared.grid_stored, 16 * (CHUNKS // 2))
                    if not (very_first and i < 2):
                        eng.wait_ge(a_ready, at - 1)
                    eng.dma_start(g_raw[i % 2][:, :, :].unsqueeze(2), src).then_inc(g_loaded[i % 2], 16)
                    if in_first(n) and i == UNROLL - 1:
                        if b:
                            y_out(b - 1)
                        if b < BLOCKS - 1:
                            if b:
                                eng.wait_ge(ss_ready, BT * b)
                            h_in(b + 1)
                    if in_last(n) and i == 0:
                        if b:
                            eng.wait_ge(y_stored, 16 * BT * b)
                        eng.dma_start(y[:, :, :], dr["x1"][b * BT:(b + 1) * BT].rearrange("t p n -> p t n"))\
                           .then_inc(x1_loaded, 16)

                each_column(eng, b, step)

            def h_in(b):
                src = dr["h2T"][b * BT:(b + 1) * BT].rearrange("t p n -> p t n")
                eng.wait_ge(h_ready, 2 * b)
                eng.dma_start(h_raw[:, :, :, :].rearrange("p t k q -> p t (k q)"), src).then_inc(h_loaded, 16)

            def y_out(b):
                for t in range(BT):
                    eng.wait_ge(y_ready, BT * b + t + 1)
                    eng.dma_start(dr["y"][b * BT + t], y[:, t, :]).then_inc(y_stored, 16)

            eng.dma_start(gain[:, :], dr["norm_final"].partition_broadcast(P)).then_inc(gain_loaded, 16)
            for b in range(BLOCKS):
                block_of_tokens(b)
            y_out(BLOCKS - 1)
            eng.wait_ge(y_stored, 16 * BT * BLOCKS)

        @block.tensor
        def _(eng):
            def scores(b, at, i):
                eng.wait_ge(u_ready, at + 1)
                n = 0
                for w, x in ((u_lo, h_hi), (u_hi, h_lo), (u_hi, h_hi)):
                    for k in range(KC):
                        mm = eng.matmul(psum[:, 6 * BANK:6 * BANK + BTOK], w[i % 2][:, k * P:(k + 1) * P],
                                        x[b % 2][:, k, :, :].rearrange("p t q -> p (t q)"),
                                        start=(n == 0), stop=(n == 3 * KC - 1))
                        n += 1
                mm.then_inc(s_done, 1)

            def grids(group):
                eng.wait_ge(onehot_ready, group + 1)
                wait_unless_0(eng, grid_ready, group)
                for n in range(GROUP):
                    out = psum[:, 7 * BANK + n * P:7 * BANK + (n + 1) * P]
                    for i in reversed(range(PARTS)):
                        mm = eng.matmul(out, rows[:, n, i, :], cols[:, n, :], start=(i == PARTS - 1), stop=(i == 0))
                mm.then_inc(grid_psum, 1)

            def outputs(b, at, i, first, last):
                eng.wait_ge(a_ready, at + 1)
                eng.wait_ge(v_ready, at + 1)
                i %= 2
                for t in range(BT):
                    if first and b:
                        eng.wait_ge(sum_ready, BT * (b - 1) + t + 1)
                    for n, (x, w) in enumerate(((a_lo, v_hi), (a_hi, v_lo), (a_hi, v_hi))):
                        for half in range(2):
                            mm = eng.matmul(psum[:, (2 * t + half) * BANK:(2 * t + half + 1) * BANK],
                                            x[i][:, t * P:(t + 1) * P], w[i][:, half * BANK:(half + 1) * BANK],
                                            start=(first and n == 0), stop=(last and n == 2))
                mm.then_inc(o_done, 1)

            def block_of_tokens(b):
                def step(n, i, group, place):
                    at = b * COLS + n * UNROLL + i
                    last = in_last(n) and i == UNROLL - 1
                    if not (last and b == BLOCKS - 1):
                        if last:
                            eng.wait_ge(h_ready, 2 * (b + 2))
                        eng.wait_ge(gl_ready, at + 1)
                        scores(b + last, at + 1, i + 1)
                    if group is not None:
                        grids(b * GROUPS + group)
                    outputs(b, at, i, in_first(n) and i == 0, last)

                each_column(eng, b, step)

            eng.wait_ge(h_ready, 2)
            scores(0, 0, 0)
            for b in range(BLOCKS):
                block_of_tokens(b)

        @block.scalar
        def _(eng):
            def split_u(c2, i):
                eng.wait_ge(u_loaded[i % 2], (c2 + i // 2 + 1) * 16)
                eng.copy(u_hi[i % 2][:, :], u_raw[i % 2][:, :]).then_inc(u_hi_ready, 1)

            def split_v(c2, i):
                eng.wait_ge(v_loaded[i % 2], (c2 + i // 2 + 1) * 16)
                eng.copy(v_hi[i % 2][:, :], v_raw[i % 2][:, :]).then_inc(v_hi_ready, 1)

            def split_h(b, half, part):
                eng.wait_ge(h_loaded, 16 * (b + 1))
                eng.copy(h_hi[b % 2][:, part, :, :], h_raw[:, :, part, :].rearrange("p t k q -> p k t q"))\
                   .then_inc(h_hi_ready, 1)

            def mean_squares(b):
                for t in range(BT):
                    eng.wait_ge(sum_ready, BT * b + t + 1)
                    eng.activation(sq[:, t, :], y[:, t, :], ACT.Square, accum_out=ss[:, t:t + 1]).then_inc(ss_ready, 1)
                eng.wait_ge(ss_ready, BT * b + BT)
                eng.activation(std[:, :], ss[:, :], ACT.Sqrt, bias=EPS, scale=1.0 / D).then_inc(std_ready, 1)

            def block_of_tokens(b):
                def step(n, i, group, place):
                    at = b * COLS + n * UNROLL + i
                    left = UNROLL - i if in_last(n) and b == BLOCKS - 1 else None
                    eng.wait_ge(s_done, at + 1)
                    eng.activation(gl[i % 2][:, :], psum[:, 6 * BANK:6 * BANK + BTOK], ACT.Gelu_apprx_tanh)\
                       .then_inc(gl_ready, 1)
                    if left not in (1, 2):
                        split_u((b * TURNS + n) * 2, i + 2)
                    if left != 1:
                        wait_unless_0(eng, o_done, at)
                        split_v((b * TURNS + n) * 2, i + 1)
                    if group is not None:
                        eng.wait_ge(grid_psum, b * GROUPS + group + 1)
                        eng.copy(grid[:, :, bass.ds(place * GROUP, GROUP)],
                                 psum[:, 7 * BANK:8 * BANK].rearrange("p (t j) -> p j t", t=GROUP))\
                           .then_inc(grid_ready, 1)
                    if in_first(n) and i == 0 and b:
                        mean_squares(b - 1)
                    if in_last(n) and i in (1, 2) and b < BLOCKS - 1:
                        split_h(b + 1, *halves()[i - 1])

                def chunk_begin(k):
                    if b == 0 and isinstance(k, int):
                        eng.wait_ge(shared.grid_stored, 16 * (CHUNKS // 2))
                    else:
                        eng.wait_ge(grid_stored, 16 * (b * CHUNKS + k))

                def chunk_end(k):
                    dst = dr["gates"][k + (b + 1) * CHUNKS]
                    eng.wait_ge(grid_ready, (b * CHUNKS + k + 1) * CHUNK_TURNS * UNROLL)
                    eng.dma_start(dst, grid[:, :, :]).then_inc(grid_stored, 16)

                each_column(eng, b, step, chunk_begin, chunk_end)

            for half, part in halves():
                split_h(0, half, part)
            split_u(0, 0)
            split_u(0, 1)
            split_v(0, 0)
            for b in range(BLOCKS):
                block_of_tokens(b)
            mean_squares(BLOCKS - 1)

        @block.vector
        def _(eng):
            def split_u(at, i):
                eng.wait_ge(u_hi_ready, at + 1)
                eng.tensor_tensor(u_lo[i % 2][:, :], u_raw[i % 2][:, :], u_hi[i % 2][:, :].bitcast(F32),
                                  ALU.subtract).then_inc(u_ready, 1)

            def split_v(at, i):
                eng.wait_ge(v_hi_ready, at + 1)
                eng.tensor_tensor(v_lo[i % 2][:, :], v_raw[i % 2][:, :], v_hi[i % 2][:, :].bitcast(F32),
                                  ALU.subtract).then_inc(v_ready, 1)

            def split_h(b, half, part):
                eng.wait_ge(h_hi_ready, 2 * b + half + 1)
                eng.tensor_tensor(h_lo[b % 2][:, part, :, :], h_raw[:, :, part, :].rearrange("p t k q -> p k t q"),
                                  h_hi[b % 2][:, part, :, :].bitcast(F32), ALU.subtract).then_inc(h_ready, 1)

            def onehots(b, group):
                wait_unless_0(eng, grid_psum, b * GROUPS + group)
                for n in range(GROUP):
                    at = b * BTOK + group * GROUP + n
                    token = at + BTOK
                    for i in range(PARTS):
                        eng.tensor_scalar(rows[:, n, i, :], iota[:, :], chosenT[:, 0, bass.ds(token, 1)],
                                          gate_part[:, i, bass.ds(at, 1)], ALU.is_equal, ALU.mult)
                    last = eng.tensor_scalar(cols[:, n, :], iota[:, :], chosenT[:, 1, bass.ds(token, 1)], None,
                                             ALU.is_equal)
                last.then_inc(onehot_ready, 1)

            def add_residual(b):
                eng.wait_ge(o_done, (b + 1) * COLS)
                eng.wait_ge(x1_loaded, 16 * (b + 1))
                for t in range(BT):
                    eng.tensor_tensor(y[:, t, :], y[:, t, :], psum[:, 2 * t * BANK:(2 * t + 2) * BANK], ALU.add)\
                       .then_inc(sum_ready, 1)

            def final_norm(b, steps):
                eng.wait_ge(std_ready, b + 1)
                eng.reciprocal(rstd[:, :], std[:, :]).then_inc(dve_step, 1)
                eng.wait_ge(dve_step, steps + 1)
                for t in range(BT):
                    eng.scalar_tensor_tensor(out=y[:, t, :], in0=y[:, t, :], scalar=rstd[:, t:t + 1], in1=gain[:, :],
                                             op0=ALU.mult, op1=ALU.mult).then_inc(y_ready, 1)

            def block_of_tokens(b):
                def step(n, i, group, place):
                    at = b * COLS + n * UNROLL + i
                    left = UNROLL - i if in_last(n) and b == BLOCKS - 1 else None
                    tail = in_first(n) and i == 0 and b
                    steps = 2 * at + (b - 1 if tail else b)
                    early = in_first(n) and i == 0 and b == 0
                    if early:
                        onehots(b, group)
                    eng.wait_ge(g_loaded[i % 2], ((b * TURNS + n) * 2 + i // 2 + 1) * 16)
                    eng.wait_ge(gl_ready, at + 1)
                    eng.tensor_tensor(a[i % 2][:, :], gl[i % 2][:, :], g_raw[i % 2][:, :, :].rearrange("p c q -> p (c q)"),
                                      ALU.mult).then_inc(dve_step, 1)
                    eng.wait_ge(dve_step, steps + 1)
                    eng.tensor_copy(a_hi[i % 2][:, :], a[i % 2][:, :]).then_inc(dve_step, 1)
                    eng.wait_ge(dve_step, steps + 2)
                    eng.tensor_tensor(a_lo[i % 2][:, :], a[i % 2][:, :], a_hi[i % 2][:, :].bitcast(F32),
                                      ALU.subtract).then_inc(a_ready, 1)
                    if tail:
                        add_residual(b - 1)
                    if left not in (1, 2):
                        split_u(at + 2, i + 2)
                    if group is not None and not early:
                        onehots(b, group)
                    if left != 1:
                        split_v(at + 1, i + 1)
                    if tail:
                        final_norm(b - 1, steps + 2)
                    if in_last(n) and i in (1, 2) and b < BLOCKS - 1:
                        split_h(b + 1, *halves()[i - 1])

                each_column(eng, b, step)

            for half, part in halves():
                split_h(0, half, part)
            split_u(0, 0)
            split_u(1, 1)
            split_v(0, 0)
            parting = Chain(eng, part_step)
            rest = chosenT[:, 2, BTOK:TOKENS]
            for i in range(PARTS - 1):
                parting.after(eng.tensor_copy(rounded[:, :], rest))
                parting.after(eng.tensor_copy(gate_part[:, i, :], rounded[:, :]))
                parting.after(eng.tensor_tensor(gate_part[:, PARTS - 1, :], rest, gate_part[:, i, :], ALU.subtract))
                rest = gate_part[:, PARTS - 1, :]
            eng.wait_ge(iota_made, 1)
            eng.wait_ge(gain_loaded, 16)
            for b in range(BLOCKS):
                block_of_tokens(b)
            add_residual(BLOCKS - 1)
            final_norm(BLOCKS - 1, 2 * BLOCKS * COLS + BLOCKS - 1)


def program(nc, dr, stages="mrge"):
    with ExitStack() as ctx:
        psum = ctx.enter_context(nc.psum_tensor("psum", [P, 8 * BANK], F32))[:, :]
        if "m" in stages:
            stage_mix(nc, psum, dr)
        if "r" in stages:
            chosenT = ctx.enter_context(nc.sbuf_tensor("chosenT_sb", [P, 3, TOKENS], F32))[:, :, :]
            stage_route(nc, psum, dr, chosenT)
            if "chosenT" in dr:
                with nc.semaphore("dbg") as dbg, nc.Block() as block:
                    @block.sync
                    def _(eng):
                        eng.dma_start(dr["chosenT"], chosenT).then_inc(dbg, 16)
                        eng.wait_ge(dbg, 16)
        if "g" in stages:
            shared = Shared(nc, ctx)
            stage_gates(nc, psum, dr, chosenT, shared)
        if "e" in stages:
            stage_experts(nc, psum, dr, chosenT, shared)


def host_inputs(inp):
    c = np.ascontiguousarray
    state = inp["state_ret"][0].reshape(STREAMS, PAIRS, 2, HD, HD)
    kc = inp["cache_swa_k"][0]
    x = np.concatenate([inp["x_prompt"].reshape(-1, D), inp["x_sample"].reshape(-1, D)]).reshape(TILES, P, D)
    return {
        "x": x,
        "xT": c(x.reshape(TILES, P, KC, P).transpose(0, 3, 2, 1)),
        "tile_tab": tile_tables(),
        "mode_tab": mode_tables(),
        "norm_mixT": c(inp["norm_mix"][0].reshape(KC, P).T),
        "norm_ffn": c(inp["norm_ffn"][0]),
        "norm_final": c(inp["norm_final"]),
        "sinks": c(inp["attn_sinks"][0].reshape(PAIRS, 2).T.reshape(HEADS)),
        "w_in": c(inp["w_in"][0]),
        "w_out": c(inp["w_out"][0]),
        "w_q": c(inp["peer_w_q"][0]),
        "keysT": c(inp["peer_keys"][0].reshape(SIDES, NKEYS, P).transpose(2, 0, 1)),
        "uT": c(inp["peer_u"][0].reshape(NKEYS, NKEYS, KC, P).transpose(1, 3, 2, 0).reshape(NKEYS, P, D)),
        "v": inp["peer_v"][0].reshape(NKEYS, NKEYS, D),
        "s0": c(state.transpose(2, 3, 1, 0, 4)),
        "kcT": c(kc.transpose(3, 2, 0, 1)),
        "kc": c(kc.reshape(STREAMS, WINDOW, KV * HD)),
        "vc": c(inp["cache_swa_v"][0].reshape(STREAMS, WINDOW, KV * HD)),
    }


OUTPUTS = {
    "y": (TILES, P, D),
    "o_sp": (HEADS, HD, HD),
    "o_kp": (P, P),
    "o_vp": (P, P),
    "o_ss": (2, HD, PAIRS, STREAMS, HD),
    "o_ks": (STREAMS, WINDOW, P),
    "o_vs": (STREAMS, WINDOW, P),
}
SCRATCH = {
    "x1": (TILES, P, D),
    "h2T": (TILES, P, D),
    "gates": (TOKENS // GATE_CHUNK, P, NKEYS, GATE_CHUNK),
}


def build(nc, arrays, stages="mrge", show=()):
    dr = {}
    for name, a in arrays.items():
        dr[name] = nc.dram_tensor(name, a.shape, mybir.dt.from_np(a.dtype), kind="ExternalInput").ap()
    for name, shape in OUTPUTS.items():
        dr[name] = nc.dram_tensor(name, shape, F32, kind="ExternalOutput").ap()
    for name, shape in SCRATCH.items():
        dr[name] = nc.dram_tensor(name, shape, F32, kind="ExternalOutput" if name in show else "Internal").ap()
    if "chosenT" in show:
        dr["chosenT"] = nc.dram_tensor("chosenT", (P, 3, TOKENS), F32, kind="ExternalOutput").ap()
    program(nc, dr, stages)


def kernel(**inputs):
    import concourse.bacc as bacc
    from concourse.bass_utils import run_bass_kernel_spmd

    arrays = host_inputs({k: np.asarray(v) for k, v in inputs.items()})
    nc = bacc.Bacc("TRN2", target_bir_lowering=False, num_devices=1)
    build(nc, arrays)
    r = run_bass_kernel_spmd(nc, [arrays], core_ids=[0]).results[0]
    y = r["y"].reshape(TOKENS, D)
    state = r["o_ss"].transpose(3, 2, 0, 1, 4).reshape(1, STREAMS, HEADS, HD, HD)
    return (
        y[:SEQ].reshape(1, SEQ, D),
        y[SEQ:].reshape(STREAMS, DEC, D),
        r["o_sp"].reshape(1, 1, HEADS, HD, HD),
        r["o_kp"].reshape(1, 1, WINDOW, KV, HD),
        r["o_vp"].reshape(1, 1, WINDOW, KV, HD),
        np.ascontiguousarray(state),
        r["o_ks"].reshape(1, STREAMS, WINDOW, KV, HD),
        r["o_vs"].reshape(1, STREAMS, WINDOW, KV, HD),
    )
```
